# Optimizing a Trainium2 kernel written in Bass

```python
import jax, jax.numpy as jnp
from jax import lax
import numpy as np

D_MODEL = 1024
BATCH = 1
SEQ = 512
DEPTH = 1

CHUNK = 128
N_SGU_GROUPS = 8
SGU_WIDTH = D_MODEL
SGU_GROUP = SGU_WIDTH // N_SGU_GROUPS
CONV_WIDTH = D_MODEL
CONV_K = 3
PROJ_WIDTHS = (SGU_WIDTH, SGU_WIDTH, CONV_WIDTH, CONV_WIDTH, CONV_WIDTH, D_MODEL, D_MODEL)
PROJ_TOTAL = sum(PROJ_WIDTHS)
PROJ_SPLITS = tuple(int(i) for i in np.cumsum(PROJ_WIDTHS)[:-1])
N_EXPERT_GROUPS = 8
EXPERTS_PER_GROUP = 8
N_EXPERTS = N_EXPERT_GROUPS * EXPERTS_PER_GROUP
TOP_K = 2
D_EXPERT = D_MODEL // 2
MOE_BLOCK = 128
EPS = 1e-6

kernel_name = "hybrid_sgu_shortconv_hiermoe_encoder"

def _rmsnorm(x, g):
    x32 = x.astype(jnp.float32)
    y = x32 * lax.rsqrt(jnp.mean(x32 * x32, axis=-1, keepdims=True) + EPS)
    return (y * g.astype(jnp.float32)).astype(x.dtype)

def _group_layernorm(v, g):
    v32 = v.astype(jnp.float32)
    mu = jnp.mean(v32, axis=-1, keepdims=True)
    d = v32 - mu
    var = jnp.mean(d * d, axis=-1, keepdims=True)
    return (d * lax.rsqrt(var + EPS) * g.astype(jnp.float32)).astype(v.dtype)

def _spatial_gate(u, v, w_s, b_s, g_ln):
    b, s, _ = v.shape
    nc = s // CHUNK
    vg = v.reshape(b, nc, CHUNK, N_SGU_GROUPS, SGU_GROUP)
    vg = _group_layernorm(vg, g_ln.reshape(N_SGU_GROUPS, SGU_GROUP))
    z = jnp.einsum('gqp,bnpgc->bnqgc', w_s, vg) + b_s.T[None, None, :, :, None]
    return u * z.reshape(b, s, SGU_WIDTH)

def _short_conv(z, w):
    s = z.shape[1]
    half = CONV_K // 2
    zp = jnp.pad(z, ((0, 0), (half, half), (0, 0)))
    out = w[0] * zp[:, 0:s]
    for k in range(1, CONV_K):
        out = out + w[k] * zp[:, k:k + s]
    return out

def _hier_moe(h, w_rg, w_re, w_gate, w_up, w_down):
    t = h.shape[0]
    g_logits = (h @ w_rg).astype(jnp.float32)
    g_prob = jax.nn.softmax(g_logits, axis=-1)
    g_idx = jnp.argmax(g_logits, axis=-1).astype(jnp.int32)
    p_g = jnp.take_along_axis(g_prob, g_idx[:, None], axis=1)
    e_logits = (h @ w_re).astype(jnp.float32).reshape(t, N_EXPERT_GROUPS, EXPERTS_PER_GROUP)
    e_logits = jnp.take_along_axis(e_logits, g_idx[:, None, None], axis=1)[:, 0]
    top_l, top_i = lax.top_k(e_logits, TOP_K)
    gate = p_g * jax.nn.softmax(top_l, axis=-1)

    eid = (g_idx[:, None] * EXPERTS_PER_GROUP + top_i).reshape(-1).astype(jnp.int32)
    tok = jnp.repeat(jnp.arange(t, dtype=jnp.int32), TOP_K)
    wt = gate.reshape(-1)
    order = jnp.argsort(eid)
    eid_s, tok_s, wt_s = eid[order], tok[order], wt[order]

    counts = jnp.bincount(eid, length=N_EXPERTS).astype(jnp.int32)
    padded = ((counts + MOE_BLOCK - 1) // MOE_BLOCK) * MOE_BLOCK
    start = jnp.cumsum(counts) - counts
    pend = jnp.cumsum(padded)
    pstart = pend - padded
    n_assign = t * TOP_K
    n_rows = -(-(n_assign + N_EXPERTS * (MOE_BLOCK - 1)) // MOE_BLOCK) * MOE_BLOCK
    n_blocks = n_rows // MOE_BLOCK

    dest = pstart[eid_s] + jnp.arange(n_assign, dtype=jnp.int32) - start[eid_s]
    row_tok = jnp.zeros((n_rows,), jnp.int32).at[dest].set(tok_s)
    row_w = jnp.zeros((n_rows,), h.dtype).at[dest].set(wt_s.astype(h.dtype))
    blk_start = jnp.arange(n_blocks, dtype=jnp.int32) * MOE_BLOCK
    blk_e = jnp.minimum(jnp.searchsorted(pend, blk_start, side='right'), N_EXPERTS - 1).astype(jnp.int32)

    xb = h[row_tok].reshape(n_blocks, MOE_BLOCK, h.shape[-1])

    def expert_block(args):
        xe, e = args
        hid = jax.nn.silu(xe @ w_gate[e]) * (xe @ w_up[e])
        return hid @ w_down[e]

    yb = lax.map(expert_block, (xb, blk_e))
    y_rows = yb.reshape(n_rows, -1) * row_w[:, None]
    return jnp.zeros_like(h).at[row_tok].add(y_rows)

def setup_inputs(seed: int = 0) -> dict:
    key = jax.random.key(seed)
    ks = jax.random.split(key, 16)
    f32 = jnp.float32
    nrm = lambda k, shape, scale: (jax.random.normal(k, shape, f32) * scale).astype(f32)
    x = jax.random.normal(ks[0], (BATCH, SEQ, D_MODEL), f32)
    g_mix = 1.0 + nrm(ks[1], (DEPTH, D_MODEL), 0.02)
    w_in = nrm(ks[2], (DEPTH, D_MODEL, PROJ_TOTAL), D_MODEL ** -0.5)
    w_s = nrm(ks[3], (DEPTH, N_SGU_GROUPS, CHUNK, CHUNK), CHUNK ** -0.5)
    b_s = 1.0 + nrm(ks[4], (DEPTH, N_SGU_GROUPS, CHUNK), 0.02)
    g_sgu = 1.0 + nrm(ks[5], (DEPTH, SGU_WIDTH), 0.02)
    w_conv = nrm(ks[6], (DEPTH, CONV_K, CONV_WIDTH), CONV_K ** -0.5)
    w_out = nrm(ks[7], (DEPTH, D_MODEL, D_MODEL), D_MODEL ** -0.5)
    g_ffn = 1.0 + nrm(ks[8], (DEPTH, D_MODEL), 0.02)
    w_router_group = nrm(ks[9], (DEPTH, D_MODEL, N_EXPERT_GROUPS), D_MODEL ** -0.5)
    w_router_expert = nrm(ks[10], (DEPTH, D_MODEL, N_EXPERTS), D_MODEL ** -0.5)
    w_gate = nrm(ks[11], (DEPTH, N_EXPERTS, D_MODEL, D_EXPERT), D_MODEL ** -0.5)
    w_up = nrm(ks[12], (DEPTH, N_EXPERTS, D_MODEL, D_EXPERT), D_MODEL ** -0.5)
    w_down = nrm(ks[13], (DEPTH, N_EXPERTS, D_EXPERT, D_MODEL), D_EXPERT ** -0.5)
    g_final = 1.0 + nrm(ks[14], (D_MODEL,), 0.02)
    return {"x": x, "g_mix": g_mix, "w_in": w_in, "w_s": w_s, "b_s": b_s,
            "g_sgu": g_sgu, "w_conv": w_conv, "w_out": w_out, "g_ffn": g_ffn,
            "w_router_group": w_router_group, "w_router_expert": w_router_expert,
            "w_gate": w_gate, "w_up": w_up, "w_down": w_down, "g_final": g_final}

def reference(x, g_mix, w_in, w_s, b_s, g_sgu, w_conv, w_out, g_ffn,
              w_router_group, w_router_expert, w_gate, w_up, w_down, g_final):
    for l in range(DEPTH):
        h = _rmsnorm(x, g_mix[l])
        proj = h @ w_in[l]
        u, v, cb, cc, xc, ga, gb = jnp.split(proj, PROJ_SPLITS, axis=-1)
        y_a = _spatial_gate(jax.nn.gelu(u), jax.nn.gelu(v), w_s[l], b_s[l], g_sgu[l])
        y_b = cb * _short_conv(cc * xc, w_conv[l])
        merged = jax.nn.sigmoid(ga) * y_a + jax.nn.sigmoid(gb) * y_b
        x = x + merged @ w_out[l]
        h2 = _rmsnorm(x, g_ffn[l]).reshape(-1, D_MODEL)
        y_moe = _hier_moe(h2, w_router_group[l], w_router_expert[l],
                          w_gate[l], w_up[l], w_down[l])
        x = x + y_moe.reshape(x.shape)
    return _rmsnorm(x, g_final)


_drawn_inputs = setup_inputs


def setup_inputs(seed=0):
    import zlib

    import numpy as np

    out = dict(_drawn_inputs(seed))
    spreads = {}
    factors = {'b_s': 5.432, 'g_sgu': 5.325, 'g_ffn': 3.337, 'g_final': 2.878}
    for name, (base, spread) in spreads.items():
        noise = np.random.default_rng([zlib.crc32(name.encode()), seed]).standard_normal(out[name].shape)
        drawn = base * np.exp(spread * noise) if base else spread * noise
        out[name] = __import__('jax').numpy.asarray(drawn.astype(out[name].dtype))
    for name, factor in factors.items():
        out[name] = (out[name] * factor).astype(out[name].dtype)
    return out
```

```python
from contextlib import ExitStack

import concourse.bass as bass
from concourse import mybir

F32 = mybir.dt.float32
F32R = mybir.dt.float32r
I32 = mybir.dt.int32
U32 = mybir.dt.uint32
ALU = mybir.AluOpType
ACT = mybir.ActivationFunctionType
AX = mybir.AxisListType

P = 128
D = 1024
T = 512
NT = T // P
NC = D // P
NJ = D // P
KINDS = 7
V_, U_, CC_, XC_, CB_, GB_, GA_ = range(KINDS)
NG = 8
NE = 64
FE = 512
NF = FE // P
CAP = 64
MAXPASS = T // CAP
UNITS = 4
UC = NC // UNITS
RING = 4
EPS = 1e-6
HALF = D // 2
OUT_OF_RANGE = 8192


def build(nc, xT, x, g_mix, w_in, w_sT, b_s, g_sgu, w_conv, w_out, g_ffn, w_rg, w_re, w_gate, w_up, w_down,
          g_final, h2_dram, y_dram, out):
    with ExitStack() as ctx:
        def sb(name, shape, dt=F32):
            return ctx.enter_context(nc.sbuf_tensor(name, shape, dt))

        def sem(name):
            return ctx.enter_context(nc.semaphore(name))

        gu_raw = sb("gu_raw", [P, 4, NC * FE])
        dn_raw = sb("dn_raw", [P, 2, NF * D])
        w_hi = sb("w_hi", [P, RING, UC * FE], F32R)
        w_lo = sb("w_lo", [P, RING, UC * FE], F32R)
        xs = sb("xs", [P, 2, NC, 2 * CAP], F32R)
        resid = sb("resid", [P, NT, D])
        arena = sb("arena", [P, KINDS, NC * P])
        w_sp = sb("w_sp", [P, NJ, P])
        b_sp = sb("b_sp", [P, NJ, P])
        zc = sb("zc", [P, T + 2])
        gffn = sb("gffn", [P, D])
        h2T = sb("h2T", [P, NC, P])
        wr = sb("wr", [P, NC, NG + NE])
        ident = sb("ident", [P, P])
        ones = sb("ones", [P, P])
        upper = sb("upper", [P, P])
        iota_e = sb("iota_e", [P, NE])
        iota_r = sb("iota_r", [P, CAP])
        member = sb("member", [P, NT, NE])
        gmix = sb("gmix", [P, NC])
        gsgu = sb("gsgu", [P, NJ])
        wconv = sb("wconv", [P, NJ, 3])
        par = sb("par", [P, 4])
        mhalf = sb("mhalf", [P, NT])
        bnst = sb("bnst", [P, NT, 6])
        bnmv = sb("bnmv", [P, NT, 2])
        lnv = sb("lnv", [P, NT])
        lnr = sb("lnr", [P, NT])
        ssq = sb("ssq", [P, NT])
        msq = sb("msq", [P, NT])
        rst = sb("rst", [P, NT])
        gmax = sb("gmax", [P, 8])
        gidx = sb("gidx", [P, 8], U32)
        gidf = sb("gidf", [P, 1])
        ngm = sb("ngm", [P, 1])
        gexp = sb("gexp", [P, NG])
        gsum_e = sb("gsum_e", [P, 1])
        gmask = sb("gmask", [P, NG])
        lg = sb("lg", [P, NG + NE])
        elm = sb("elm", [P, NE])
        el8 = sb("el8", [P, 8])
        em8 = sb("em8", [P, 8])
        ei8 = sb("ei8", [P, 8], U32)
        eif = sb("eif", [P, 2])
        e2 = sb("e2", [P, 1])
        den = sb("den", [P, 1])
        rden = sb("rden", [P, 1])
        eid = sb("eid", [P, NT, 2])
        onehot = sb("onehot", [P, 2, NE])
        rank = sb("rank", [P, NT, 2])
        gate_w = sb("gate_w", [P, NT, 2])
        idv = sb("idv", [P, NT, 2])
        cmax = sb("cmax", [P, 1])
        thr = sb("thr", [P, MAXPASS])
        thrm = sb("thrm", [P, MAXPASS])
        npf = sb("npf", [P, 1])
        npi = sb("npi", [P, 1], I32)
        tb_v = sb("tb_v", [CAP, NE])
        tb_e = sb("tb_e", [CAP, NE])
        tok_tab = sb("tok_tab", [CAP, NE], U32)
        id_tab = sb("id_tab", [CAP, NE], U32)
        gat_idx = sb("gat_idx", [CAP, 2], U32)
        sca_idx = sb("sca_idx", [CAP, 2], U32)
        scratch = sb("scratch", [P, NE])

        hT = dn_raw[:, 1, :].rearrange("p (c t) -> p c t", c=NC)
        h2p = dn_raw[:, 1, :].rearrange("p (t c q) -> p t c q", t=NT, c=NC)
        merged = gu_raw[:, 3, :].rearrange("p (k t) -> p k t", k=NJ)
        tmp = resid[:, :, :].rearrange("p a (b t) -> p (a b) t", b=2)
        g_v, g_u, c_c, t_b, t_a, cnv, a_z, vhat = (tmp[:, i, :] for i in range(8))
        sq_slots = [tmp[:, 0, :], tmp[:, 1, :]]
        v_all = w_sp[:, 0:4, :].rearrange("p a (b e) -> p (a b) e", e=NE)
        r_all = w_sp[:, 4:8, :].rearrange("p a (b e) -> p (a b) e", e=CAP)
        work = arena[:, :, :].rearrange("p a b -> p (a b)")
        xg = [work[0:CAP, 0:D], work[0:CAP, D:2 * D]]
        ye = [work[0:CAP, 2 * D:3 * D], work[0:CAP, 3 * D:4 * D]]
        g_low, u_low, g_sum, u_sum, g_act, hid = (work[0:CAP, 4 * D + i * FE:4 * D + (i + 1) * FE] for i in range(6))
        hidT = b_sp[:, 0:2, :].rearrange("p a (b r) -> p (a b) r", r=CAP)
        sq_dump = zc[:, 0:T].bitcast(mybir.dt.bfloat16)
        w_in_slot = [arena[:, k, :].rearrange("p (c n) -> p c n", c=NC) for k in range(KINDS)]
        wo = [arena[:, k, :] for k in range(KINDS)] + [b_sp[:, :, :].rearrange("p a b -> p (a b)")]

        bank = [ctx.enter_context(nc.psum_tensor(f"bank{i}", [P, 512], F32))[:, :] for i in range(4)]
        y_ps = ctx.enter_context(nc.psum_tensor("y_ps", [P, 1024], F32))
        bank += [y_ps[:, 0:512], y_ps[:, 512:1024]]
        bank += [ctx.enter_context(nc.psum_tensor(f"bank{i}", [P, 512], F32))[:, :] for i in (6, 7)]

        xT_in, small_in, wr_in, x_in = sem("xT_in"), sem("small_in"), sem("wr_in"), sem("x_in")
        w_in_in = [sem(f"w_in_in{k}") for k in range(KINDS + 1)]
        gu_in = [sem(f"gu_in{k}") for k in range(4)]
        dn_in = [sem(f"dn_in{k}") for k in range(2)]
        consts = sem("consts")
        squared, squares_used, ms_ps, rms_a, rms_b, rms_c = (sem(n) for n in
            ("squared", "squares_used", "ms_ps", "rms_a", "rms_b", "rms_c"))
        h_ready = sem("h_ready")
        proj_done, v_gelu, u_gelu, cc_copied, tanh_b, tanh_a = (sem(n) for n in
            ("proj_done", "v_gelu", "u_gelu", "cc_copied", "tanh_b", "tanh_a"))
        vT_done, z_done = sem("vT_done"), sem("z_done")
        par_ready, stats, aggr, var_eps, ln_rstd, vhat_ready = (sem(n) for n in
            ("par_ready", "stats", "aggr", "var_eps", "ln_rstd", "vhat_ready"))
        conv_in, conv0, conv1, conv2, yb_done, zb_done, az_done, b_gated, a_gated, merged_done = (sem(n) for n in
            ("conv_in", "conv0", "conv1", "conv2", "yb_done", "zb_done", "az_done", "b_gated", "a_gated",
             "merged_done"))
        o_done, x2_ready, ssq_ready, msq_ready, rst_ready, h2_ready, h2_stored = (sem(n) for n in
            ("o_done", "x2_ready", "ssq_ready", "msq_ready", "rst_ready", "h2_ready", "h2_stored"))
        h2T_ps, h2T_ready, logits, routed, gexp_done, e2_done, member_ready, prefix_done = (sem(n) for n in
            ("h2T_ps", "h2T_ready", "logits", "routed", "gexp_done", "e2_done", "member_ready", "prefix_done"))
        ngm_ready, e2_ready, rstep = sem("ngm_ready"), sem("e2_ready"), sem("rstep")
        np_ready, rv_ready, tab_ps, tab_step, tab_ready, xg_clear = (sem(n) for n in
            ("np_ready", "rv_ready", "tab_ps", "tab_step", "tab_ready", "xg_clear"))
        gidx_copied, sidx_copied = sem("gidx_copied"), sem("sidx_copied")
        gathered = [sem(f"gathered{s}") for s in range(2)]
        scattered = [sem(f"scattered{s}") for s in range(2)]
        xT_done = [sem(f"xT_done{s}") for s in range(2)]
        xhi_done, xlo_done = sem("xhi_done"), sem("xlo_done")
        hi_done = [sem(f"hi_done{k}") for k in range(2 * UNITS)]
        lo_done = [sem(f"lo_done{k}") for k in range(2 * UNITS)]
        unit_used = [sem(f"unit_used{k}") for k in range(2 * UNITS)]
        g_low_ready, u_low_ready, g_act_ready, hid_ready = (sem(n) for n in
            ("g_low_ready", "u_low_ready", "g_act_ready", "hid_ready"))
        g_summed = [sem(f"g_summed{s}") for s in range(2)]
        u_summed = [sem(f"u_summed{s}") for s in range(2)]
        hidT_ps, hidT_ready = sem("hidT_ps"), sem("hidT_ready")
        down_done = [sem(f"down_done{h}") for h in range(2)]
        ye_ready = [sem(f"ye_ready{h}") for h in range(2)]
        ye_free = [sem(f"ye_free{s}") for s in range(2)]
        pass_closed = sem("pass_closed")
        y_in = [sem(f"y_in{t}") for t in range(NT)]
        gf_in = sem("gf_in")
        comb0, comb1, fsq, fms, frs, out_ready, out_stored = (sem(n) for n in
            ("comb0", "comb1", "fsq", "fms", "frs", "out_ready", "out_stored"))

        def passes(eng):
            eng.wait_ge(np_ready, 1)
            return eng.value_load(npi[0:1, 0:1], min_val=1, max_val=MAXPASS)

        block = ctx.enter_context(nc.Block())

        @block.sync
        def _(sp):
            sp.dma_start(hT[:, :, :], xT).then_inc(xT_in, 16)
            for k in range(KINDS):
                sp.dma_start(arena[:, k, :], w_in[0, :, k, :]).then_inc(w_in_in[k], 16)

            def load_gate_up(e, pair, s, half):
                w = (w_gate, w_up)[half]
                sp.dma_start(gu_raw[:, 2 * s + half, :], w[bass.ds(e, 1)].rearrange("o (p c) f -> (o p) (c f)", c=NC)
                             if not isinstance(e, int) else w[e].rearrange("(p c) f -> p (c f)", c=NC)
                             ).then_inc(gu_in[2 * s + half], 16)

            def load_down(e, s):
                src = (w_down[bass.ds(e, 1)].rearrange("o (c p) d -> (o p) c d", p=P)
                       if not isinstance(e, int) else w_down[e].rearrange("(c p) d -> p c d", p=P))
                sp.dma_start(dn_raw[:, s, :].rearrange("p (c d) -> p c d", c=NF), src).then_inc(dn_in[s], 16)

            load_gate_up(0, 0, 0, 0)
            load_gate_up(0, 0, 0, 1)
            load_down(0, 0)
            load_gate_up(1, 0, 1, 0)
            with sp.Fori(1, NJ) as j:
                for k in range(KINDS):
                    sp.wait_ge(proj_done, KINDS * j - KINDS + k + 1)
                    sp.dma_start(arena[:, k, :], w_in[bass.ds(j, 1), :, k, :].rearrange("o p n -> (o p) n")
                                 ).then_inc(w_in_in[k], 16)
            for k in range(KINDS):
                sp.wait_ge(proj_done, KINDS * (NJ - 1) + k + 1)
                sp.dma_start(wo[k], w_out[k]).then_inc(w_in_in[k], 16)
            sp.wait_ge(zb_done, NJ + 1)
            sp.dma_start(wo[NC - 1], w_out[NC - 1]).then_inc(w_in_in[KINDS], 16)
            sp.wait_ge(merged_done, NJ + 1)
            sp.dma_start(resid[:, :, :], x).then_inc(x_in, 16)
            for t in range(NT):
                sp.wait_ge(h2_ready, t + 1)
                sp.dma_start(h2_dram[t * P:(t + 1) * P, :], h2p[:, t, :, :].rearrange("p c q -> p (c q)")
                             ).then_inc(h2_stored, 16)
            sp.wait_ge(o_done, 2 * NT)
            load_gate_up(1, 0, 1, 1)
            sp.wait_ge(h2_stored, 16 * NT)
            sp.wait_ge(h2T_ps, 2 * NT)
            load_down(1, 1)

            def load_block(e, n, s):
                sp.wait_ge(lo_done[UNITS - 1], n - 1)
                load_gate_up(e, 0, s, 0)
                sp.wait_ge(lo_done[2 * UNITS - 1], n - 1)
                load_gate_up(e, 0, s, 1)
                sp.wait_ge(down_done[1], n)
                load_down(e, s)

            with sp.Fori(1, NE // 2) as i:
                for s in range(2):
                    load_block(2 * i + s, 2 * i + s, s)
            n_pass = passes(sp)
            with sp.If(n_pass > 1):
                with sp.Fori(1, n_pass) as p:
                    with sp.Fori(0, NE // 2) as i:
                        for s in range(2):
                            load_block(2 * i + s, NE * p + 2 * i + s, s)
            scatters, blocks = sp.to_reg(16 * (NE // 2) * n_pass), sp.to_reg(NE * n_pass + 1)
            sp.wait_ge(np_ready, 1)
            for s in range(2):
                sp.wait_ge(scattered[s], scatters)
            sp.wait_ge(down_done[1], blocks)
            sp.dma_start(dn_raw[:, 0, 0:D], g_final.partition_broadcast(P)).then_inc(gf_in, 16)
            for t in range(NT):
                sp.dma_start(gu_raw[:, t, 0:2 * D].rearrange("p (k d) -> p k d", k=2),
                             y_dram.rearrange("(k t) d -> t k d", k=2)[t * P:(t + 1) * P]).then_inc(y_in[t], 16)
            for t in range(NT):
                sp.wait_ge(out_ready, t + 1)
                sp.dma_start(out[t * P:(t + 1) * P, :], dn_raw[:, 1, t * D:(t + 1) * D]).then_inc(out_stored, 16)
            sp.wait_ge(out_stored, 16 * NT)

        @block.gpsimd
        def _(pool):
            for s_ in (*ye_free, pass_closed):
                pool.sem_inc(s_, 1)
            pool.memset(ones[:], 1.0).then_inc(consts, 1)
            pool.memset(zc[:], 0.0).then_inc(consts, 1)
            pool.memset(mhalf[:], -0.5).then_inc(consts, 1)
            pool.wait_ge(consts, 3)
            pool.affine_select(ident[:], ones[:], pattern=[[-1, P]], compare_op=ALU.is_equal, fill=0.0, base=0,
                               channel_multiplier=1).then_inc(consts, 1)
            pool.affine_select(upper[:], ones[:], pattern=[[1, P]], compare_op=ALU.is_gt, fill=0.0, base=0,
                               channel_multiplier=-1).then_inc(consts, 1)
            pool.iota(iota_e[:], pattern=[[1, NE]], base=0, channel_multiplier=0,
                      allow_small_or_imprecise_dtypes=True).then_inc(consts, 1)
            pool.iota(iota_r[:], pattern=[[1, CAP]], base=0, channel_multiplier=0,
                      allow_small_or_imprecise_dtypes=True).then_inc(consts, 1)
            pool.iota(idv[:].rearrange("p t k -> p (t k)"), pattern=[[P, NT], [T, 2]], base=1, channel_multiplier=1,
                      allow_small_or_imprecise_dtypes=True).then_inc(consts, 1)
            pool.iota(thr[:], pattern=[[CAP, MAXPASS]], base=0, channel_multiplier=0,
                      allow_small_or_imprecise_dtypes=True).then_inc(consts, 1)
            with pool.Fori(0, NJ) as j:
                pool.wait_ge(var_eps, j + 1)
                pool.tensor_tensor(lnr[:], lnv[:], mhalf[:], ALU.pow).then_inc(ln_rstd, 1)
            for t in range(NT):
                pool.wait_ge(msq_ready, t + 1)
                pool.tensor_tensor(rst[:, t:t + 1], msq[:, t:t + 1], mhalf[:, 0:1], ALU.pow).then_inc(rst_ready, 1)
            pool.wait_ge(o_done, 2 * NT)
            for s in range(2):
                pool.memset(xg[s], 0.0).then_inc(xg_clear, 1)
            pool.wait_ge(xg_clear, 2)
            pool.wait_ge(h2_stored, 16 * NT)

            def gather(b, n, i, s):
                n_1, freed = pool.to_reg(n + 1), pool.to_reg(i + 1)
                pool.wait_ge(np_ready, 1)
                pool.wait_ge(xT_done[s], freed)
                pool.tensor_copy(gat_idx[:, s:s + 1], tok_tab[:, bass.ds(b, 1)] if not isinstance(b, int)
                                 else tok_tab[:, b:b + 1]).then_inc(gidx_copied, 1)
                pool.wait_ge(h2_stored, 16 * NT)
                pool.wait_ge(gidx_copied, n_1)
                pool.indirect_dma_start(xg[s], None, h2_dram,
                                        bass.IndirectOffsetOnAxis(ap=gat_idx[:, s:s + 1], axis=0),
                                        bounds_check=T - 1, oob_is_err=False).then_inc(gathered[s], 16)

            def scatter(b, n, i, s):
                n_1, n_2 = pool.to_reg(n + 1), pool.to_reg(n + 2)
                pool.tensor_copy(sca_idx[:, s:s + 1], id_tab[:, bass.ds(b, 1)] if not isinstance(b, int)
                                 else id_tab[:, b:b + 1]).then_inc(sidx_copied, 1)
                pool.wait_ge(np_ready, 1)
                pool.wait_ge(sidx_copied, n_1)
                for h in range(2):
                    pool.wait_ge(ye_ready[h], n_2)
                pool.indirect_dma_start(y_dram, bass.IndirectOffsetOnAxis(ap=sca_idx[:, s:s + 1], axis=0), ye[s],
                                        None, bounds_check=2 * T - 1, oob_is_err=False).then_inc(scattered[s], 16)

            def free_rows(i, s):
                landed = pool.to_reg(16 * i + 16)
                pool.wait_ge(np_ready, 1)
                pool.wait_ge(scattered[s], landed)
                pool.sem_inc(ye_free[s], 1)

            n_pass = passes(pool)
            with pool.Fori(0, n_pass) as p:
                n0, i0 = NE * p, (NE // 2) * p
                tables = pool.to_reg(2 * p + 2)
                pool.wait_ge(np_ready, 1)
                pool.wait_ge(tab_ready, tables)
                for k in range(5):
                    gather(k, n0 + k, i0 + k // 2, k % 2)
                scatter(0, n0, i0, 0)
                with pool.Fori(0, NE // 2 - 3) as i:
                    gather(2 * i + 5, n0 + 2 * i + 5, i0 + i + 2, 1)
                    scatter(2 * i + 1, n0 + 2 * i + 1, i0 + i, 1)
                    free_rows(i0 + i, 0)
                    gather(2 * i + 6, n0 + 2 * i + 6, i0 + i + 3, 0)
                    scatter(2 * i + 2, n0 + 2 * i + 2, i0 + i + 1, 0)
                    free_rows(i0 + i, 1)
                gather(NE - 1, n0 + NE - 1, i0 + NE // 2 - 1, 1)
                for k in range(NE - 5, NE):
                    scatter(k, n0 + k, i0 + k // 2, k % 2)
                    free_rows(i0 + (k - 1) // 2, (k - 1) % 2)
                free_rows(i0 + NE // 2 - 1, 1)
                pool.sem_inc(pass_closed, 1)
            for t in range(NT):
                pool.wait_ge(fms, t + 1)
                pool.tensor_tensor(rst[:, t:t + 1], msq[:, t:t + 1], mhalf[:, 0:1], ALU.pow).then_inc(frs, 1)

        @block.tensor
        def _(pe):
            for s_ in (vT_done, z_done, *xT_done, *unit_used, hidT_ps, *down_done):
                pe.sem_inc(s_, 1)
            pe.wait_ge(consts, 9)
            for c in range(NC):
                pe.wait_ge(squared, c + 1)
                pe.matmul(bank[7], ones[:], sq_slots[c % 2], start=(c == 0), stop=(c == NC - 1)
                          ).then_inc(squares_used, 1)

            def project(j, k, first=False):
                for c in range(NC):
                    last = pe.matmul(bank[k], w_in_slot[k][:, c, :], hT[:, c, :],
                                     start=(c == 0), stop=(c == NC - 1))
                last.then_inc(proj_done, 1)

            pe.wait_ge(h_ready, NC)
            with pe.Fori(0, NJ) as j:
                pe.wait_ge(w_in_in[V_], 16 * j + 16)
                pe.wait_ge(zb_done, j + 1)
                project(j, V_)
                pe.wait_ge(w_in_in[U_], 16 * j + 16)
                pe.wait_ge(u_gelu, j + 1)
                project(j, U_)
                pe.wait_ge(v_gelu, j + 1)
                pe.wait_ge(vhat_ready, j + 1)
                for n in range(NT):
                    last = pe.transpose(bank[7][:, n * P:(n + 1) * P], g_v[:, n * P:(n + 1) * P], ident[:])
                last.then_inc(vT_done, 1)
                pe.wait_ge(w_in_in[CC_], 16 * j + 16)
                pe.wait_ge(cc_copied, j + 1)
                project(j, CC_)
                pe.wait_ge(vhat_ready, j + 2)
                for n in range(NT):
                    last = pe.matmul(bank[0][:, n * P:(n + 1) * P], vhat[:, n * P:(n + 1) * P],
                                     w_sp[:, bass.ds(j, 1), :].rearrange("p o q -> p (o q)"), start=True, stop=True)
                last.then_inc(z_done, 1)
                for k, free in ((XC_, conv_in), (CB_, yb_done), (GB_, tanh_b), (GA_, tanh_a)):
                    pe.wait_ge(w_in_in[k], 16 * j + 16)
                    pe.wait_ge(free, j + 1)
                    project(j, k)

            def out_proj(t):
                for h in range(2):
                    if t >= 2:
                        pe.wait_ge(x2_ready, 2 * (t - 2) + h + 1)
                    for k in range(NC):
                        if t == 0 and h == 0:
                            pe.wait_ge(w_in_in[k], 16 * (NJ + 1) if k < KINDS else 16)
                            if k == 0:
                                pe.wait_ge(merged_done, NJ + 1)
                        last = pe.matmul(bank[2 * (t % 2) + h], merged[:, k, t * P:(t + 1) * P],
                                         wo[k][:, h * HALF:(h + 1) * HALF], start=(k == 0), stop=(k == NC - 1))
                    last.then_inc(o_done, 1)

            def router(t):
                pe.wait_ge(h2_ready, t + 1)
                for h in range(2):
                    if t >= 1:
                        pe.wait_ge(h2T_ready, 2 * t - 1 + h)
                    for c in range(4):
                        last = pe.transpose(bank[4 + h][:, c * P:(c + 1) * P], h2p[:, t, 4 * h + c, :], ident[:])
                    last.then_inc(h2T_ps, 1)
                if t == 0:
                    pe.wait_ge(wr_in, 32)
                if t >= 1:
                    pe.wait_ge(routed, t)
                for c in range(NC):
                    if c % 4 == 0:
                        pe.wait_ge(h2T_ready, 2 * t + c // 4 + 1)
                    last = pe.matmul(bank[6][:, 0:NG + NE], h2T[:, c, :], wr[:, c, :], start=(c == 0), stop=(c == NC - 1))
                last.then_inc(logits, 1)

            def prefix(t):
                pe.wait_ge(member_ready, t + 1)
                for q in range(t + 1):
                    last = pe.matmul(bank[7][:, t * NE:(t + 1) * NE], upper[:] if q == t else ones[:], member[:, q, :],
                                     start=(q == 0), stop=(q == t))
                if t == NT - 1:
                    for q in range(NT):
                        last = pe.matmul(bank[7][:, NT * NE:(NT + 1) * NE], ones[:], member[:, q, :],
                                         start=(q == 0), stop=(q == NT - 1))
                last.then_inc(prefix_done, 1)

            out_proj(0)
            out_proj(1)
            router(0)
            out_proj(2)
            prefix(0)
            router(1)
            out_proj(3)
            prefix(1)
            router(2)
            prefix(2)
            router(3)
            prefix(3)

            def transpose_rows(i, s):
                landed = pe.to_reg(16 * i + 16)
                pe.wait_ge(consts, 9)
                pe.wait_ge(gathered[s], landed)
                for c in range(NC):
                    last = pe.transpose(bank[6][:, c * CAP:(c + 1) * CAP], xg[s][:, c * P:(c + 1) * P],
                                        ident[0:CAP, 0:CAP])
                last.then_inc(xT_done[s], 1)

            def product(n, s, half, b):
                for u in range(UNITS):
                    k = half * UNITS + u
                    pe.wait_ge(lo_done[k], n + 1)
                    for c in range(UC):
                        for part in (w_hi, w_lo):
                            last = pe.matmul(bank[b], xs[:, s, u * UC + c, :],
                                             part[:, k % RING, c * FE:(c + 1) * FE],
                                             start=(u == 0 and c == 0 and part is w_hi),
                                             stop=(u == UNITS - 1 and c == UC - 1 and part is w_lo))
                    last.then_inc(unit_used[k], 1)

            def hid_transposes(n):
                hid_n, copied = pe.to_reg(n + 2), pe.to_reg(n + 1)
                pe.wait_ge(consts, 9)
                pe.wait_ge(hid_ready, hid_n)
                pe.wait_ge(hidT_ready, copied)
                for c in range(NF):
                    last = pe.transpose(bank[7][:, c * CAP:(c + 1) * CAP], hid[:, c * P:(c + 1) * P],
                                        ident[0:CAP, 0:CAP])
                last.then_inc(hidT_ps, 1)

            def down(n, i, s):
                pe.wait_ge(hidT_ready, n + 2)
                pe.wait_ge(dn_in[s], 16 * i + 16)
                for h in range(2):
                    pe.wait_ge(ye_ready[h], n + 1)
                    for c in range(NF):
                        last = pe.matmul(bank[4 + h][0:CAP, :], hidT[:, c, :],
                                         dn_raw[:, s, c * D + h * HALF:c * D + (h + 1) * HALF],
                                         start=(c == 0), stop=(c == NF - 1))
                    last.then_inc(down_done[h], 1)

            def pe_block(n, i, s, has_prev, has_next, i_prev, i_next):
                pe.wait_ge(xlo_done, n + 2)
                pe.wait_ge(g_summed[s], i + 1)
                product(n, s, 0, s)
                if has_next:
                    transpose_rows(i_next, 1 - s)
                if has_prev:
                    hid_transposes(n - 1)
                pe.wait_ge(u_summed[s], i + 1)
                product(n, s, 1, 2 + s)
                if has_prev:
                    down(n - 1, i_prev, 1 - s)

            n_pass = passes(pe)
            with pe.Fori(0, n_pass) as p:
                n0, i0 = NE * p, (NE // 2) * p
                pe.wait_ge(rv_ready, p + 1)
                for q in range(2 * NT):
                    last = pe.matmul(bank[7][0:CAP, 0:NE], r_all[:, q, :], v_all[:, q, :], start=(q == 0),
                                     stop=(q == 2 * NT - 1))
                last.then_inc(tab_ps, 1)
                pe.wait_ge(xlo_done, n0 + 1)
                transpose_rows(i0, 0)
                pe.wait_ge(tab_ready, 2 * p + 2)
                pe_block(n0, i0, 0, False, True, None, i0)
                with pe.Fori(0, NE // 2 - 1) as i:
                    pe_block(n0 + 2 * i + 1, i0 + i, 1, True, True, i0 + i, i0 + i + 1)
                    pe_block(n0 + 2 * i + 2, i0 + i + 1, 0, True, True, i0 + i, i0 + i + 1)
                pe_block(n0 + NE - 1, i0 + NE // 2 - 1, 1, True, False, i0 + NE // 2 - 1, None)
                hid_transposes(n0 + NE - 1)
                down(n0 + NE - 1, i0 + NE // 2 - 1, 1)

        @block.scalar
        def _(act):
            for s_ in (u_gelu, cc_copied, tanh_b, tanh_a, hidT_ready, g_act_ready, ye_ready[0]):
                act.sem_inc(s_, 1)
            act.dma_start(gmix[:], g_mix).then_inc(small_in, 16)
            act.dma_start(gsgu[:], g_sgu).then_inc(small_in, 16)
            act.dma_start(wconv[:, :, :], w_conv).then_inc(small_in, 16)
            act.dma_start(w_sp[:, :, :], w_sT).then_inc(small_in, 16)
            act.dma_start(b_sp[:, :, :].rearrange("p g q -> p (g q)"), b_s.partition_broadcast(P)
                          ).then_inc(small_in, 16)
            act.dma_start(gffn[:], g_ffn.partition_broadcast(P)).then_inc(small_in, 16)
            act.dma_start(wr[:, :, 0:NG], w_rg.rearrange("(p c) g -> p c g", c=NC)).then_inc(wr_in, 16)
            act.dma_start(wr[:, :, NG:NG + NE], w_re.rearrange("(p c) g -> p c g", c=NC)).then_inc(wr_in, 16)

            act.wait_ge(xT_in, 16)
            for c in range(NC):
                if c >= 2:
                    act.wait_ge(squares_used, c - 1)
                act.activation(sq_slots[c % 2], hT[:, c, :], ACT.Square).then_inc(squared, 1)
            act.wait_ge(rms_a, 1)
            act.activation(a_z, c_c, ACT.Sqrt).then_inc(rms_b, 1)

            with act.Fori(0, NJ) as j:
                act.wait_ge(proj_done, KINDS * j + V_ + 1)
                act.wait_ge(vT_done, j + 1)
                act.activation(g_v, bank[0], ACT.Gelu_apprx_tanh).then_inc(v_gelu, 1)
                act.wait_ge(merged_done, j + 1)
                act.wait_ge(proj_done, KINDS * j + U_ + 1)
                act.activation(g_u, bank[1], ACT.Gelu_apprx_tanh).then_inc(u_gelu, 1)
                act.wait_ge(proj_done, KINDS * j + CC_ + 1)
                act.activation(c_c, bank[2], ACT.Copy).then_inc(cc_copied, 1)
                act.wait_ge(proj_done, KINDS * j + GB_ + 1)
                act.activation(t_b, bank[5], ACT.Tanh, scale=0.5).then_inc(tanh_b, 1)
                act.wait_ge(proj_done, KINDS * j + GA_ + 1)
                act.activation(t_a, bank[6], ACT.Tanh, scale=0.5).then_inc(tanh_a, 1)

            def act_square(t):
                act.wait_ge(x2_ready, 2 * t + 2)
                if t >= 1:
                    act.wait_ge(ssq_ready, t)
                act.activation(sq_dump, resid[:, t, :], ACT.Square, accum_out=ssq[:, t:t + 1]
                               ).then_inc(ssq_ready, 1)

            def act_router(t):
                for h in range(2):
                    act.wait_ge(h2T_ps, 2 * t + h + 1)
                    if t >= 1 and h == 0:
                        act.wait_ge(logits, t)
                    act.activation(h2T[:, 4 * h:4 * h + 4, :].rearrange("p c q -> p (c q)"),
                                   bank[4 + h], ACT.Copy).then_inc(h2T_ready, 1)
                act.wait_ge(ngm_ready, t + 1)
                act.activation(gexp[:], lg[:, 0:NG], ACT.Exp, bias=ngm[:], accum_out=gsum_e[:]).then_inc(gexp_done, 1)
                act.wait_ge(e2_ready, t + 1)
                act.activation(e2[:], eif[:, 0:1], ACT.Exp).then_inc(e2_done, 1)

            act_square(0)
            act_square(1)
            act_router(0)
            act_square(2)
            act_router(1)
            act_square(3)
            act_router(2)
            act_router(3)

            def hi_unit(n, i, s, half, u):
                k = half * UNITS + u
                if u == 0:
                    act.wait_ge(gu_in[2 * s + half], 16 * i + 16)
                if k >= RING:
                    act.wait_ge(unit_used[k - RING], n + 2)
                else:
                    act.wait_ge(unit_used[k + RING], n + 1)
                act.activation(w_hi[:, k % RING, :], gu_raw[:, 2 * s + half, u * UC * FE:(u + 1) * UC * FE],
                               ACT.Copy).then_inc(hi_done[k], 1)

            def x_hi(n, i, s):
                act.wait_ge(xT_done[s], i + 2)
                act.activation(xs[:, s, :, 0:CAP], bank[6].rearrange("p (c r) -> p c r", c=NC), ACT.Copy
                               ).then_inc(xhi_done, 1)

            def hid_copy(n):
                act.wait_ge(hidT_ps, n + 2)
                act.wait_ge(down_done[1], n + 1)
                act.activation(hidT[:, :, :].rearrange("p c r -> p (c r)"), bank[7][:, 0:NF * CAP], ACT.Copy
                               ).then_inc(hidT_ready, 1)

            def y_half(n, i, s):
                act.wait_ge(down_done[0], n + 2)
                act.wait_ge(ye_free[s], i + 1)
                act.activation(ye[s][:, 0:HALF], bank[4][0:CAP, :], ACT.Copy).then_inc(ye_ready[0], 1)

            def act_block(n, i, s, has_prev, has_next, i_prev, i_next):
                for u in range(UNITS):
                    hi_unit(n, i, s, 1, u)
                act.wait_ge(unit_used[UNITS - 1], n + 2)
                if has_prev:
                    act.wait_ge(g_summed[1 - s], i_prev + 2)
                act.activation(g_low, bank[s][CAP:2 * CAP, :], ACT.Copy).then_inc(g_low_ready, 1)
                if has_next:
                    x_hi(n + 1, i_next, 1 - s)
                if has_prev:
                    hid_copy(n - 1)
                if has_next:
                    hi_unit(n + 1, i_next, 1 - s, 0, 0)
                act.wait_ge(g_summed[s], i + 2)
                act.wait_ge(hid_ready, n + 1)
                act.activation(g_act, g_sum, ACT.Silu).then_inc(g_act_ready, 1)
                if has_next:
                    for u in range(1, UNITS):
                        hi_unit(n + 1, i_next, 1 - s, 0, u)
                act.wait_ge(unit_used[2 * UNITS - 1], n + 2)
                if has_prev:
                    act.wait_ge(u_summed[1 - s], i_prev + 2)
                act.activation(u_low, bank[2 + s][CAP:2 * CAP, :], ACT.Copy).then_inc(u_low_ready, 1)
                if has_prev:
                    y_half(n - 1, i_prev, 1 - s)

            n_pass = passes(act)
            with act.Fori(0, n_pass) as p:
                n0, i0 = NE * p, (NE // 2) * p
                x_hi(n0, i0, 0)
                for u in range(UNITS):
                    hi_unit(n0, i0, 0, 0, u)
                act_block(n0, i0, 0, False, True, None, i0)
                with act.Fori(0, NE // 2 - 1) as i:
                    act_block(n0 + 2 * i + 1, i0 + i, 1, True, True, i0 + i, i0 + i + 1)
                    act_block(n0 + 2 * i + 2, i0 + i + 1, 0, True, True, i0 + i, i0 + i + 1)
                act_block(n0 + NE - 1, i0 + NE // 2 - 1, 1, True, False, i0 + NE // 2 - 1, None)
                hid_copy(n0 + NE - 1)
                y_half(n0 + NE - 1, i0 + NE // 2 - 1, 1)

            for t in range(NT):
                act.wait_ge(comb1, t + 1)
                if t >= 1:
                    act.wait_ge(fsq, t)
                act.activation(sq_dump, resid[:, t, :], ACT.Square, accum_out=ssq[:, t:t + 1]).then_inc(fsq, 1)

        @block.vector
        def _(dve):
            for s_ in (zb_done, vhat_ready, conv_in, yb_done, merged_done, xlo_done, *g_summed, *u_summed, hid_ready, ye_ready[1]):
                dve.sem_inc(s_, 1)
            dve.wait_ge(squares_used, NC)
            dve.tensor_scalar(c_c, bank[7], 1.0 / D, EPS, ALU.mult, ALU.add).then_inc(rms_a, 1)
            dve.wait_ge(rms_b, 1)
            dve.reciprocal(t_b, a_z).then_inc(rms_c, 1)
            dve.wait_ge(rms_c, 1)
            dve.wait_ge(small_in, 96)
            for c in range(NC):
                dve.scalar_tensor_tensor(hT[:, c, :], hT[:, c, :], gmix[:, c:c + 1], t_b, ALU.mult, ALU.mult
                                         ).then_inc(h_ready, 1)

            with dve.Fori(0, NJ) as j:
                dve.tensor_copy(par[:, 0:3], wconv[:, bass.ds(j, 1), :].rearrange("p o k -> p (o k)")
                                ).then_inc(par_ready, 1)
                dve.tensor_copy(par[:, 3:4], gsgu[:, bass.ds(j, 1)]).then_inc(par_ready, 1)
                dve.wait_ge(vT_done, j + 2)
                for n in range(NT):
                    last = dve.bn_stats(bnst[:, n, :], bank[7][:, n * P:(n + 1) * P])
                last.then_inc(stats, 1)
                stats_j = dve.to_reg(j + 1)
                dve.wait_ge(consts, 9)
                dve.wait_ge(stats, stats_j)
                for n in range(NT):
                    last = dve.bn_aggr(bnmv[:, n, :], bnst[:, n, :])
                last.then_inc(aggr, 1)
                dve.wait_ge(aggr, j + 1)
                dve.tensor_scalar(lnv[:], bnmv[:, :, 1], EPS, None, ALU.add).then_inc(var_eps, 1)
                dve.wait_ge(ln_rstd, j + 1)
                dve.wait_ge(z_done, j + 1)
                for n in range(NT):
                    last = dve.tensor_scalar(vhat[:, n * P:(n + 1) * P], bank[7][:, n * P:(n + 1) * P],
                                             bnmv[:, n, 0:1], lnr[:, n:n + 1], ALU.subtract, ALU.mult)
                last.then_inc(vhat_ready, 1)
                dve.wait_ge(z_done, j + 2)
                dve.wait_ge(par_ready, 2 * j + 2)
                for n in range(NT):
                    last = dve.scalar_tensor_tensor(a_z[:, n * P:(n + 1) * P], bank[0][:, n * P:(n + 1) * P],
                                                    par[:, 3:4],
                                                    b_sp[:, bass.ds(j, 1), :].rearrange("p o q -> p (o q)"),
                                                    ALU.mult, ALU.add)
                last.then_inc(zb_done, 1)
                dve.wait_ge(zb_done, j + 2)
                dve.wait_ge(u_gelu, j + 2)
                dve.tensor_tensor(a_z, a_z, g_u, ALU.mult).then_inc(az_done, 1)
                dve.wait_ge(cc_copied, j + 2)
                dve.wait_ge(proj_done, KINDS * j + XC_ + 1)
                dve.tensor_tensor(zc[:, 1:T + 1], bank[3], c_c, ALU.mult).then_inc(conv_in, 1)
                dve.wait_ge(conv_in, j + 2)
                dve.tensor_scalar(cnv, zc[:, 0:T], par[:, 0:1], None, ALU.mult).then_inc(conv0, 1)
                dve.wait_ge(conv0, j + 1)
                dve.scalar_tensor_tensor(cnv, zc[:, 1:T + 1], par[:, 1:2], cnv, ALU.mult, ALU.add).then_inc(conv1, 1)
                dve.wait_ge(conv1, j + 1)
                dve.scalar_tensor_tensor(cnv, zc[:, 2:T + 2], par[:, 2:3], cnv, ALU.mult, ALU.add).then_inc(conv2, 1)
                dve.wait_ge(conv2, j + 1)
                dve.wait_ge(proj_done, KINDS * j + CB_ + 1)
                dve.tensor_tensor(cnv, bank[4], cnv, ALU.mult).then_inc(yb_done, 1)
                dve.wait_ge(yb_done, j + 2)
                dve.wait_ge(tanh_b, j + 2)
                dve.scalar_tensor_tensor(cnv, t_b, 1.0, cnv, ALU.add, ALU.mult).then_inc(b_gated, 1)
                dve.wait_ge(az_done, j + 1)
                dve.wait_ge(tanh_a, j + 2)
                dve.scalar_tensor_tensor(a_z, t_a, 1.0, a_z, ALU.add, ALU.mult).then_inc(a_gated, 1)
                dve.wait_ge(b_gated, j + 1)
                dve.wait_ge(a_gated, j + 1)
                dve.tensor_tensor(merged[:, bass.ds(j, 1), :].rearrange("p o t -> p (o t)"), a_z, cnv, ALU.add
                                  ).then_inc(merged_done, 1)

            step = [0]

            def link(ins):
                step[0] += 1
                ins.then_inc(rstep, 1)
                dve.wait_ge(rstep, step[0])

            def residual(t):
                if t == 0:
                    dve.wait_ge(x_in, 16)
                for h in range(2):
                    dve.wait_ge(o_done, 2 * t + h + 1)
                    dve.scalar_tensor_tensor(resid[:, t, h * HALF:(h + 1) * HALF], bank[2 * (t % 2) + h], 0.5,
                                             resid[:, t, h * HALF:(h + 1) * HALF], ALU.mult, ALU.add
                                             ).then_inc(x2_ready, 1)
                dve.wait_ge(ssq_ready, t + 1)
                dve.tensor_scalar(msq[:, t:t + 1], ssq[:, t:t + 1], 1.0 / D, EPS, ALU.mult, ALU.add
                                  ).then_inc(msq_ready, 1)
                dve.wait_ge(rst_ready, t + 1)
                dve.scalar_tensor_tensor(h2p[:, t, :, :].rearrange("p c q -> p q c"),
                                         resid[:, t, :].rearrange("p (q c) -> p q c", c=NC), rst[:, t:t + 1],
                                         gffn[:].rearrange("p (q c) -> p q c", c=NC), ALU.mult, ALU.mult
                                         ).then_inc(h2_ready, 1)

            def route(t):
                dve.wait_ge(logits, t + 1)
                if t >= 1:
                    dve.wait_ge(e2_done, t)
                link(dve.tensor_copy(lg[:], bank[6][:, 0:NG + NE]))
                link(dve.max(gmax[:], lg[:, 0:NG]))
                dve.tensor_scalar(ngm[:], gmax[:, 0:1], -1.0, None, ALU.mult).then_inc(ngm_ready, 1)
                link(dve.max_index(gidx[:], gmax[:], lg[:, 0:NG]))
                link(dve.tensor_copy(gidf[:], gidx[:, 0:1]))
                link(dve.tensor_scalar(gmask[:], iota_e[:, 0:NG], gidf[:], None, ALU.is_equal))
                link(dve.tensor_tensor(elm[:].rearrange("p (g e) -> p g e", g=NG),
                                       lg[:, NG:NG + NE].rearrange("p (g e) -> p g e", g=NG),
                                       gmask[:].unsqueeze(2).to_broadcast([P, NG, NE // NG]), ALU.mult))
                link(dve.tensor_reduce(el8[:], elm[:].rearrange("p (g e) -> p e g", g=NG), AX.X, ALU.add))
                link(dve.max(em8[:], el8[:]))
                link(dve.max_index(ei8[:], em8[:], el8[:]))
                link(dve.tensor_copy(eif[:], ei8[:, 0:2]))
                link(dve.scalar_tensor_tensor(eid[:, t, :], gidf[:].to_broadcast([P, 2]), float(NE // NG), eif[:],
                                              ALU.mult, ALU.add))
                for k in range(2):
                    link(dve.tensor_scalar(onehot[:, k, :], iota_e[:], eid[:, t, k:k + 1], None, ALU.is_equal))
                dve.tensor_tensor(member[:, t, :], onehot[:, 0, :], onehot[:, 1, :], ALU.add
                                  ).then_inc(member_ready, 1)
                dve.tensor_tensor(eif[:, 0:1], em8[:, 1:2], em8[:, 0:1], ALU.subtract).then_inc(e2_ready, 1)
                for k in range(2):
                    link(dve.tensor_scalar(v_all[:, 2 * t + k, :], iota_e[:], eid[:, t, k:k + 1], idv[:, t, k:k + 1],
                                           ALU.is_equal, ALU.mult))
                dve.wait_ge(gexp_done, t + 1)
                dve.wait_ge(e2_done, t + 1)
                link(dve.tensor_scalar(den[:], e2[:], 1.0, gsum_e[:], ALU.add, ALU.mult))
                link(dve.reciprocal(gate_w[:, t, 0:1], den[:]))
                dve.wait_ge(prefix_done, t + 1)
                link(dve.tensor_tensor(gate_w[:, t, 1:2], gate_w[:, t, 0:1], e2[:], ALU.mult))
                for k in range(2):
                    link(dve.tensor_tensor_reduce(scratch[:], bank[7][:, t * NE:(t + 1) * NE], onehot[:, k, :],
                                                  1.0, 0.0, ALU.mult, ALU.add, rank[:, t, k:k + 1]))
                last_of_tile = dve.tensor_copy(rden[:], den[:])
                last_of_tile.then_inc(routed, 1)

            residual(0)
            residual(1)
            route(0)
            residual(2)
            route(1)
            residual(3)
            route(2)
            route(3)
            link(dve.tensor_reduce(cmax[:], bank[7][:, NT * NE:(NT + 1) * NE], AX.X, ALU.max))
            link(dve.tensor_scalar(thrm[:], thr[:], cmax[:], None, ALU.is_lt))
            link(dve.tensor_reduce(npf[:], thrm[:], AX.X, ALU.add))
            dve.tensor_copy(npi[:], npf[:]).then_inc(np_ready, 1)

            def lo_unit(n, i, s, half, u):
                k = half * UNITS + u
                dve.wait_ge(hi_done[k], n + 1)
                dve.tensor_tensor(w_lo[:, k % RING, :], gu_raw[:, 2 * s + half, u * UC * FE:(u + 1) * UC * FE],
                                  w_hi[:, k % RING, :].bitcast(F32), ALU.subtract).then_inc(lo_done[k], 1)

            def x_lo(n, s):
                dve.wait_ge(xhi_done, n + 1)
                dve.tensor_tensor(xs[:, s, :, CAP:2 * CAP], bank[6].rearrange("p (c r) -> p c r", c=NC),
                                  xs[:, s, :, 0:CAP].bitcast(F32), ALU.subtract).then_inc(xlo_done, 1)

            def y_half(n, i, s):
                dve.wait_ge(down_done[1], n + 2)
                dve.wait_ge(ye_free[s], i + 1)
                dve.tensor_copy(ye[s][:, HALF:D], bank[5][0:CAP, :]).then_inc(ye_ready[1], 1)

            def dve_block(n, i, s, has_prev, has_next, i_prev, i_next):
                for u in range(UNITS):
                    lo_unit(n, i, s, 1, u)
                dve.wait_ge(g_low_ready, n + 1)
                dve.wait_ge(g_act_ready, n + 1)
                dve.tensor_tensor(g_sum, bank[s][0:CAP, :], g_low, ALU.add).then_inc(g_summed[s], 1)
                if has_next:
                    x_lo(n + 1, 1 - s)
                    for u in range(UNITS):
                        lo_unit(n + 1, i_next, 1 - s, 0, u)
                dve.wait_ge(u_low_ready, n + 1)
                dve.tensor_tensor(u_sum, bank[2 + s][0:CAP, :], u_low, ALU.add).then_inc(u_summed[s], 1)
                dve.wait_ge(u_summed[s], i + 2)
                dve.wait_ge(g_act_ready, n + 2)
                dve.wait_ge(hidT_ps, n + 1)
                dve.tensor_tensor(hid, u_sum, g_act, ALU.mult).then_inc(hid_ready, 1)
                if has_prev:
                    y_half(n - 1, i_prev, 1 - s)

            n_pass = passes(dve)
            with dve.Fori(0, n_pass) as p:
                n0, i0 = NE * p, (NE // 2) * p
                for q in range(2 * NT):
                    last = dve.tensor_scalar(r_all[:, q, :], iota_r[:], rank[:, q // 2, q % 2:q % 2 + 1], None,
                                             ALU.is_equal)
                last.then_inc(rv_ready, 1)
                dve.wait_ge(rv_ready, p + 1)
                dve.tensor_scalar(iota_r[:], iota_r[:], float(CAP), None, ALU.add).then_inc(tab_step, 1)
                dve.wait_ge(tab_ps, p + 1)
                dve.tensor_copy(tb_v[:], bank[7][0:CAP, 0:NE]).then_inc(tab_step, 1)
                dve.wait_ge(tab_step, 5 * p + 2)
                dve.tensor_scalar(tb_e[:], tb_v[:], 0.5, float(OUT_OF_RANGE), ALU.is_lt, ALU.mult).then_inc(tab_step, 1)
                dve.wait_ge(tab_step, 5 * p + 3)
                dve.scalar_tensor_tensor(tb_v[:], tb_v[:], -1.0, tb_e[:], ALU.add, ALU.add).then_inc(tab_step, 1)
                dve.wait_ge(tab_step, 5 * p + 4)
                dve.wait_ge(pass_closed, p + 1)
                dve.tensor_scalar(tb_e[:], tb_v[:], float(T) - 0.5, -float(T), ALU.is_gt, ALU.mult
                                  ).then_inc(tab_step, 1)
                dve.tensor_copy(id_tab[:], tb_v[:]).then_inc(tab_ready, 1)
                dve.wait_ge(tab_step, 5 * p + 5)
                dve.tensor_tensor(tok_tab[:], tb_v[:], tb_e[:], ALU.add).then_inc(tab_ready, 1)
                dve.wait_ge(xlo_done, n0 + 1)
                x_lo(n0, 0)
                for u in range(UNITS):
                    lo_unit(n0, i0, 0, 0, u)
                dve_block(n0, i0, 0, False, True, None, i0)
                with dve.Fori(0, NE // 2 - 1) as i:
                    dve_block(n0 + 2 * i + 1, i0 + i, 1, True, True, i0 + i, i0 + i + 1)
                    dve_block(n0 + 2 * i + 2, i0 + i + 1, 0, True, True, i0 + i, i0 + i + 1)
                dve_block(n0 + NE - 1, i0 + NE // 2 - 1, 1, True, False, i0 + NE // 2 - 1, None)
                y_half(n0 + NE - 1, i0 + NE // 2 - 1, 1)

            dve.wait_ge(gf_in, 16)

            def combine(t):
                dve.wait_ge(y_in[t], 16)
                dve.scalar_tensor_tensor(resid[:, t, :], gu_raw[:, t, 0:D], gate_w[:, t, 0:1], resid[:, t, :],
                                         ALU.mult, ALU.add).then_inc(comb0, 1)
                dve.wait_ge(comb0, t + 1)
                dve.scalar_tensor_tensor(resid[:, t, :], gu_raw[:, t, D:2 * D], gate_w[:, t, 1:2], resid[:, t, :],
                                         ALU.mult, ALU.add).then_inc(comb1, 1)

            def finish(t):
                dve.wait_ge(fsq, t + 1)
                dve.tensor_scalar(msq[:, t:t + 1], ssq[:, t:t + 1], 1.0 / D, EPS, ALU.mult, ALU.add).then_inc(fms, 1)
                dve.wait_ge(frs, t + 1)
                dve.scalar_tensor_tensor(dn_raw[:, 1, t * D:(t + 1) * D], resid[:, t, :], rst[:, t:t + 1],
                                         dn_raw[:, 0, 0:D], ALU.mult, ALU.mult).then_inc(out_ready, 1)

            combine(0)
            for t in range(NT):
                if t + 1 < NT:
                    combine(t + 1)
                finish(t)


_ORDER = (1, 0, 3, 4, 2, 6, 5)


def kernel(x, g_mix, w_in, w_s, b_s, g_sgu, w_conv, w_out, g_ffn, w_router_group, w_router_expert, w_gate, w_up,
           w_down, g_final):
    import numpy as np
    import concourse.bacc as bacc
    from concourse.bass_utils import run_bass_kernel_spmd

    x = np.asarray(x)
    arrays = {
        "xT": np.asarray(x)[0].T.reshape(P, NC, T),
        "x": x[0].reshape(NT, P, D).transpose(1, 0, 2),
        "g_mix": np.asarray(g_mix).reshape(P, NC),
        "w_in": np.asarray(w_in)[0].reshape(P, NC, KINDS, NJ, P)[:, :, list(_ORDER)].transpose(3, 0, 2, 1, 4)
                .reshape(NJ, P, KINDS, NC * P),
        "w_sT": np.asarray(w_s)[0].transpose(2, 0, 1),
        "b_s": np.asarray(b_s).reshape(NJ * P),
        "g_sgu": np.asarray(g_sgu).reshape(NJ, P).T,
        "w_conv": np.asarray(w_conv)[0].reshape(3, NJ, P).transpose(2, 1, 0),
        "w_out": np.asarray(w_out)[0].reshape(NC, P, D),
        "g_ffn": np.asarray(g_ffn).reshape(D),
        "w_rg": np.asarray(w_router_group)[0],
        "w_re": np.asarray(w_router_expert)[0],
        "w_gate": np.asarray(w_gate)[0],
        "w_up": np.asarray(w_up)[0],
        "w_down": np.asarray(w_down)[0],
        "g_final": np.asarray(g_final).reshape(D),
    }
    nc = bacc.Bacc("TRN2", target_bir_lowering=False, num_devices=1)
    feed, aps = {}, {}
    for name, a in arrays.items():
        feed["in_" + name] = np.ascontiguousarray(a)
        aps[name] = nc.dram_tensor("in_" + name, a.shape, F32, kind="ExternalInput").ap()
    h2_dram = nc.dram_tensor("h2_rows", (T, D), F32, kind="Internal").ap()
    y_dram = nc.dram_tensor("y_rows", (2 * T, D), F32, kind="Internal").ap()
    out = nc.dram_tensor("out_0", (T, D), F32, kind="ExternalOutput").ap()
    build(nc, **aps, h2_dram=h2_dram, y_dram=y_dram, out=out)
    r = run_bass_kernel_spmd(nc, [feed], core_ids=[0])
    return r.results[0]["out_0"].reshape(1, T, D)
```

```python
from contextlib import ExitStack

import concourse.bass as bass
from concourse import mybir

F32 = mybir.dt.float32
F32R = mybir.dt.float32r
I32 = mybir.dt.int32
U32 = mybir.dt.uint32
ALU = mybir.AluOpType
ACT = mybir.ActivationFunctionType
AX = mybir.AxisListType

P = 128
D = 1024
T = 512
NT = T // P
NC = D // P
NJ = D // P
KINDS = 7
V_, U_, CC_, XC_, CB_, GB_, GA_ = range(KINDS)
NG = 8
NE = 64
FE = 512
NF = FE // P
CAP = 64
MAXPASS = T // CAP
UNITS = 4
UC = NC // UNITS
RING = 4
EPS = 1e-6
HALF = D // 2
OUT_OF_RANGE = 8192


def build(nc, xT, x, g_mix, w_in, w_sT, b_s, g_sgu, w_conv, w_out, g_ffn, w_rg, w_re, w_gate, w_up, w_down,
          g_final, h2_dram, y_dram, out):
    with ExitStack() as ctx:
        def sb(name, shape, dt=F32):
            return ctx.enter_context(nc.sbuf_tensor(name, shape, dt))

        def sem(name):
            return ctx.enter_context(nc.semaphore(name))

        def sb_both(name, shape):
            offset = -(-nc.sbuf_base // 32) * 32
            return sb(name, shape), nc.alloc_sbuf_tensor_at(name + "_r", shape, F32R, offset=offset)

        gu_raw, gu_raw_r = sb_both("gu_raw", [P, 4, NC * FE])
        dn_raw, dn_raw_r = sb_both("dn_raw", [P, 2, NF * D])
        arena, arena_r = sb_both("arena", [P, KINDS, NC * P])
        b_sp, b_sp_r = sb_both("b_sp", [P, NJ, P])
        w_hi = sb("w_hi", [P, RING, UC * FE], F32R)
        w_lo = sb("w_lo", [P, RING, UC * FE], F32R)
        xs = sb("xs", [P, 2, NC, 2 * CAP], F32R)
        resid = sb("resid", [P, NT, D])
        w_sp = sb("w_sp", [P, NJ, P])
        zc = sb("zc", [P, T + 2])
        m_lo_b = sb("m_lo_b", [P, NJ // 2, T], F32R)
        wr = sb("wr", [P, NC, NG + NE])
        ident = sb("ident", [P, P])
        ones = sb("ones", [P, P])
        upper = sb("upper", [P, P])
        iota_e = sb("iota_e", [P, NE])
        iota_r = sb("iota_r", [P, CAP])
        member = sb("member", [P, NT, NE])
        gmix = sb("gmix", [P, NC])
        gsgu = sb("gsgu", [P, NJ])
        wconv = sb("wconv", [P, NJ, 3])
        par = sb("par", [P, 4])
        mhalf = sb("mhalf", [P, NT])
        bnst = sb("bnst", [P, NT, 6])
        bnmv = sb("bnmv", [P, NT, 2])
        lnv = sb("lnv", [P, NT])
        lnr = sb("lnr", [P, NT])
        ssq = sb("ssq", [P, NT])
        msq = sb("msq", [P, NT])
        rst = sb("rst", [P, NT])
        gmax = sb("gmax", [P, 8])
        gidx = sb("gidx", [P, 8], U32)
        gidf = sb("gidf", [P, 1])
        ngm = sb("ngm", [P, 1])
        gexp = sb("gexp", [P, NG])
        gsum_e = sb("gsum_e", [P, 1])
        gmask = sb("gmask", [P, NG])
        lg = sb("lg", [P, NG + NE])
        elm = sb("elm", [P, NE])
        el8 = sb("el8", [P, 8])
        em8 = sb("em8", [P, 8])
        ei8 = sb("ei8", [P, 8], U32)
        eif = sb("eif", [P, 2])
        e2 = sb("e2", [P, 1])
        den = sb("den", [P, 1])
        rden = sb("rden", [P, 1])
        eid = sb("eid", [P, NT, 2])
        onehot = sb("onehot", [P, 2, NE])
        rank = sb("rank", [P, NT, 2])
        gate_w = sb("gate_w", [P, NT, 2])
        idv = sb("idv", [P, NT, 2])
        cmax = sb("cmax", [P, 1])
        thr = sb("thr", [P, MAXPASS])
        thrm = sb("thrm", [P, MAXPASS])
        npf = sb("npf", [P, 1])
        npi = sb("npi", [P, 1], I32)
        tb_v = sb("tb_v", [CAP, NE])
        tb_e = sb("tb_e", [CAP, NE])
        tok_tab = sb("tok_tab", [CAP, NE], U32)
        id_tab = sb("id_tab", [CAP, NE], U32)
        gat_idx = sb("gat_idx", [CAP, 2], U32)
        sca_idx = sb("sca_idx", [CAP, 2], U32)
        scratch = sb("scratch", [P, NE])

        h_raw = gu_raw[:, 2, :].rearrange("p (c t) -> p c t", c=NC)
        h_lo = gu_raw_r[:, 2, :].rearrange("p (c t) -> p c t", c=NC)
        h_hi = dn_raw_r[:, 1, :].rearrange("p (c t) -> p c t", c=NC)
        h2p = dn_raw[:, 1, :].rearrange("p (t c q) -> p t c q", t=NT, c=NC)
        m_hi = gu_raw_r[:, 3, :].rearrange("p (k t) -> p k t", k=NJ)
        m_lo_a = xs[:, :, :, :].rearrange("p s c r -> p (s c r)").rearrange("p (k t) -> p k t", t=T)
        m_lo = [(m_lo_a if k < NJ // 2 else m_lo_b)[:, k % (NJ // 2), :] for k in range(NJ)]
        g_fin = gu_raw[:, 0, 2 * D:3 * D]
        h2T = gu_raw[:, 2, 0:D].rearrange("p (c q) -> p c q", c=NC)
        gffn = gu_raw[:, 2, D:2 * D]
        tmp = resid[:, :, :].rearrange("p a (b t) -> p (a b) t", b=2)
        g_v, g_u, c_c, t_b, t_a, cnv, a_z, vhat = (tmp[:, i, :] for i in range(8))
        squares = [tmp[:, c, :] for c in range(NC)]
        sq_sum = squares[0]
        rms_all = tmp[:, 1, :]
        rms_diag = tmp[:, 2, :].rearrange("p (n q) -> p n q", n=NT)
        v_all = w_sp[:, 0:4, :].rearrange("p a (b e) -> p (a b) e", e=NE)
        r_all = w_sp[:, 4:8, :].rearrange("p a (b e) -> p (a b) e", e=CAP)
        work = arena[:, :, :].rearrange("p a b -> p (a b)")
        xg = [work[0:CAP, 0:D], work[0:CAP, D:2 * D]]
        ye = [work[0:CAP, 2 * D:3 * D], work[0:CAP, 3 * D:4 * D]]
        g_low, u_low, g_sum, u_sum, g_act, hid = (work[0:CAP, 4 * D + i * FE:4 * D + (i + 1) * FE] for i in range(6))
        hidT = b_sp[:, 0:2, :].rearrange("p a (b r) -> p (a b) r", r=CAP)
        sq_dump = zc[:, 0:T].bitcast(mybir.dt.bfloat16)
        in_hi = [w_hi[:, k, :] for k in range(RING)] + [w_lo[:, k, :] for k in range(RING)]
        in_raw = [arena[:, k, :] for k in range(KINDS)] + [b_sp[:, :, :].rearrange("p a b -> p (a b)")]
        in_lo = [arena_r[:, k, :] for k in range(KINDS)] + [b_sp_r[:, :, :].rearrange("p a b -> p (a b)")]

        bank = [ctx.enter_context(nc.psum_tensor(f"bank{i}", [P, 512], F32))[:, :] for i in range(4)]
        y_ps = ctx.enter_context(nc.psum_tensor("y_ps", [P, 1024], F32))
        bank += [y_ps[:, 0:512], y_ps[:, 512:1024]]
        bank += [ctx.enter_context(nc.psum_tensor(f"bank{i}", [P, 512], F32))[:, :] for i in (6, 7)]

        xT_in = [sem(f"xT_in{q}") for q in range(NC // 2)]
        gmix_in, small_in, wr_in, x_in = sem("gmix_in"), sem("small_in"), sem("wr_in"), sem("x_in")
        w_in_in = [sem(f"w_in_in{k}") for k in range(KINDS + 1)]
        gu_in = [sem(f"gu_in{k}") for k in range(4)]
        dn_in = [sem(f"dn_in{k}") for k in range(4)]
        consts = sem("consts")
        squared, squares_summed, ms_summed, ms_ready, rms_ready, diag_ready, rms_spread = (sem(n) for n in
            ("squared", "squares_summed", "ms_summed", "ms_ready", "rms_ready", "diag_ready", "rms_spread"))
        h_ready = [sem(f"h_ready_{w}") for w in ("even", "odd")]
        gmix_applied = sem("gmix_applied")
        rms_copied, h_hi_done, h_lo_done = sem("rms_copied"), sem("h_hi_done"), sem("h_lo_done")
        in_hi_done, in_lo_done = sem("in_hi_done"), sem("in_lo_done")
        proj_done, v_gelu, u_gelu, cc_copied, tanh_b, tanh_a = (sem(n) for n in
            ("proj_done", "v_gelu", "u_gelu", "cc_copied", "tanh_b", "tanh_a"))
        vT_done, z_done = sem("vT_done"), sem("z_done")
        par_ready, stats, aggr, var_eps, ln_rstd, vhat_ready = (sem(n) for n in
            ("par_ready", "stats", "aggr", "var_eps", "ln_rstd", "vhat_ready"))
        m_hi_done, m_lo_done, gffn_in, logits_read = (sem(n) for n in
            ("m_hi_done", "m_lo_done", "gffn_in", "logits_read"))
        conv_in, conv0, conv1, conv2, yb_done, zb_done, az_done, b_gated, a_gated, merged_done = (sem(n) for n in
            ("conv_in", "conv0", "conv1", "conv2", "yb_done", "zb_done", "az_done", "b_gated", "a_gated",
             "merged_done"))
        o_done, x2_ready, ssq_ready, msq_ready, rst_ready, h2_ready, h2_stored = (sem(n) for n in
            ("o_done", "x2_ready", "ssq_ready", "msq_ready", "rst_ready", "h2_ready", "h2_stored"))
        h2T_ps, h2T_ready, logits, routed, gexp_done, e2_done, member_ready, prefix_done = (sem(n) for n in
            ("h2T_ps", "h2T_ready", "logits", "routed", "gexp_done", "e2_done", "member_ready", "prefix_done"))
        ngm_ready, e2_ready, rstep = sem("ngm_ready"), sem("e2_ready"), sem("rstep")
        np_ready, rv_ready, tab_ps, tab_step, tab_ready, xg_clear = (sem(n) for n in
            ("np_ready", "rv_ready", "tab_ps", "tab_step", "tab_ready", "xg_clear"))
        gidx_copied, sidx_copied = sem("gidx_copied"), sem("sidx_copied")
        gathered = [sem(f"gathered{s}") for s in range(2)]
        scattered = [sem(f"scattered{s}") for s in range(2)]
        xT_done = [sem(f"xT_done{s}") for s in range(2)]
        xhi_done, xlo_done = sem("xhi_done"), sem("xlo_done")
        hi_done = [sem(f"hi_done{k}") for k in range(2 * UNITS)]
        lo_done = [sem(f"lo_done{k}") for k in range(2 * UNITS)]
        unit_used = [sem(f"unit_used{k}") for k in range(2 * UNITS)]
        g_low_ready, u_low_ready, g_act_ready, hid_ready = (sem(n) for n in
            ("g_low_ready", "u_low_ready", "g_act_ready", "hid_ready"))
        g_summed = [sem(f"g_summed{s}") for s in range(2)]
        u_summed = [sem(f"u_summed{s}") for s in range(2)]
        hidT_ps, hidT_ready = sem("hidT_ps"), sem("hidT_ready")
        down_done = [sem(f"down_done{h}") for h in range(2)]
        ye_ready = [sem(f"ye_ready{h}") for h in range(2)]
        ye_free = [sem(f"ye_free{s}") for s in range(2)]
        pass_closed = sem("pass_closed")
        y_in = [sem(f"y_in{t}") for t in range(NT)]
        gf_in = sem("gf_in")
        comb0, comb1, fsq, fms, frs, out_ready, out_stored = (sem(n) for n in
            ("comb0", "comb1", "fsq", "fms", "frs", "out_ready", "out_stored"))

        def passes(eng):
            eng.wait_ge(np_ready, 1)
            return eng.value_load(npi[0:1, 0:1], min_val=1, max_val=MAXPASS)

        block = ctx.enter_context(nc.Block())

        @block.sync
        def _(sp):
            for q in range(NC // 2):
                sp.dma_start(h_raw[:, 2 * q:2 * q + 2, :], xT[:, 2 * q:2 * q + 2, :]).then_inc(xT_in[q], 16)
                if q == 0:
                    sp.dma_start(gmix[:], g_mix).then_inc(gmix_in, 16)
            for k in range(KINDS):
                sp.dma_start(arena[:, k, :], w_in[0, :, k, :]).then_inc(w_in_in[k], 16)
                if k == U_:
                    sp.dma_start(gsgu[:], g_sgu).then_inc(small_in, 16)
                    sp.dma_start(wconv[:, :, :], w_conv).then_inc(small_in, 16)
                    sp.dma_start(w_sp[:, :, :], w_sT).then_inc(small_in, 16)
                    sp.dma_start(b_sp[:, :, :].rearrange("p g q -> p (g q)"), b_s.partition_broadcast(P)
                                 ).then_inc(small_in, 16)
            sp.dma_start(wr[:, :, 0:NG], w_rg.rearrange("(p c) g -> p c g", c=NC)).then_inc(wr_in, 16)
            sp.dma_start(wr[:, :, NG:NG + NE], w_re.rearrange("(p c) g -> p c g", c=NC)).then_inc(wr_in, 16)

            def load_gate_up(e, s, half):
                w = (w_gate, w_up)[half]
                sp.dma_start(gu_raw[:, 2 * s + half, :], w[bass.ds(e, 1)].rearrange("o (p c) f -> (o p) (c f)", c=NC)
                             if not isinstance(e, int) else w[e].rearrange("(p c) f -> p (c f)", c=NC)
                             ).then_inc(gu_in[2 * s + half], 16)

            def load_down(e, s):
                for half in range(2):
                    src = (w_down[bass.ds(e, 1)].rearrange("o (c p) d -> (o p) c d", p=P)
                           if not isinstance(e, int) else w_down[e].rearrange("(c p) d -> p c d", p=P))
                    cs = slice(half * NF // 2, (half + 1) * NF // 2)
                    sp.dma_start(dn_raw[:, s, :].rearrange("p (c d) -> p c d", c=NF)[:, cs, :], src[:, cs, :]
                                 ).then_inc(dn_in[2 * s + half], 16)

            load_gate_up(0, 0, 0)
            load_gate_up(0, 0, 1)
            load_down(0, 0)
            with sp.Fori(1, NJ) as j:
                for k in range(KINDS):
                    sp.wait_ge(proj_done, KINDS * j - KINDS + k + 1)
                    sp.dma_start(arena[:, k, :], w_in[bass.ds(j, 1), :, k, :].rearrange("o p n -> (o p) n")
                                 ).then_inc(w_in_in[k], 16)
            for k in range(KINDS):
                if k == XC_:
                    sp.wait_ge(zb_done, NJ + 1)
                    sp.dma_start(in_raw[NC - 1], w_out[NC - 1]).then_inc(w_in_in[KINDS], 16)
                sp.wait_ge(proj_done, KINDS * (NJ - 1) + k + 1)
                sp.dma_start(in_raw[k], w_out[k]).then_inc(w_in_in[k], 16)
            sp.dma_start(gffn, g_ffn.partition_broadcast(P)).then_inc(gffn_in, 16)
            sp.wait_ge(m_lo_done, NJ)
            sp.dma_start(resid[:, :, :], x).then_inc(x_in, 16)
            for t in range(NT):
                sp.wait_ge(h2_ready, t + 1)
                sp.dma_start(h2_dram[t * P:(t + 1) * P, :], h2p[:, t, :, :].rearrange("p c q -> p (c q)")
                             ).then_inc(h2_stored, 16)
            sp.wait_ge(o_done, 2 * NT)
            load_gate_up(1, 1, 1)
            sp.wait_ge(h2_stored, 16 * NT)
            sp.wait_ge(h2T_ps, 2 * NT)
            load_down(1, 1)
            sp.wait_ge(logits, NT)
            load_gate_up(1, 1, 0)

            def load_next_gate_up(e, n, s):
                sp.wait_ge(lo_done[UNITS - 1], n - 1)
                load_gate_up(e, s, 0)
                sp.wait_ge(lo_done[2 * UNITS - 1], n - 1)
                load_gate_up(e, s, 1)

            def load_next_down(e, n, s):
                sp.wait_ge(down_done[1], n)
                load_down(e, s)

            load_next_gate_up(2, 2, 0)
            load_next_gate_up(3, 3, 1)
            load_next_down(2, 2, 0)
            with sp.Fori(2, NE // 2) as i:
                for s in range(2):
                    n = 2 * i + s
                    load_next_gate_up(n, n, s)
                    load_next_down(n - 1, n - 1, 1 - s)
            load_next_down(NE - 1, NE - 1, 1)
            n_pass = passes(sp)
            with sp.If(n_pass > 1):
                with sp.Fori(1, n_pass) as p:
                    n0 = NE * p
                    load_next_gate_up(0, n0, 0)
                    load_next_gate_up(1, n0 + 1, 1)
                    load_next_down(0, n0, 0)
                    with sp.Fori(1, NE // 2) as i:
                        for s in range(2):
                            load_next_gate_up(2 * i + s, n0 + 2 * i + s, s)
                            load_next_down(2 * i + s - 1, n0 + 2 * i + s - 1, 1 - s)
                    load_next_down(NE - 1, n0 + NE - 1, 1)
            scatters, blocks = sp.to_reg(16 * (NE // 2) * n_pass), sp.to_reg(NE * n_pass)
            sp.wait_ge(np_ready, 1)
            sp.wait_ge(lo_done[2 * UNITS - 1], blocks)
            sp.dma_start(g_fin, g_final.partition_broadcast(P)).then_inc(gf_in, 16)
            sp.wait_ge(np_ready, 1)
            for s in range(2):
                sp.wait_ge(scattered[s], scatters)
            for t in range(NT):
                sp.dma_start(gu_raw[:, t, 0:2 * D].rearrange("p (k d) -> p k d", k=2),
                             y_dram.rearrange("(k t) d -> t k d", k=2)[t * P:(t + 1) * P]).then_inc(y_in[t], 16)
            for t in range(NT):
                sp.wait_ge(out_ready, t + 1)
                sp.dma_start(out[t * P:(t + 1) * P, :], dn_raw[:, 1, t * D:(t + 1) * D]).then_inc(out_stored, 16)
            sp.wait_ge(out_stored, 16 * NT)

        @block.gpsimd
        def _(pool):
            for s_ in (*ye_free, pass_closed):
                pool.sem_inc(s_, 1)
            pool.memset(ones[:], 1.0).then_inc(consts, 1)
            pool.memset(zc[:], 0.0).then_inc(consts, 1)
            pool.memset(mhalf[:], -0.5).then_inc(consts, 1)
            pool.wait_ge(consts, 3)
            pool.affine_select(ident[:], ones[:], pattern=[[-1, P]], compare_op=ALU.is_equal, fill=0.0, base=0,
                               channel_multiplier=1).then_inc(consts, 1)
            pool.affine_select(upper[:], ones[:], pattern=[[1, P]], compare_op=ALU.is_gt, fill=0.0, base=0,
                               channel_multiplier=-1).then_inc(consts, 1)
            pool.iota(iota_e[:], pattern=[[1, NE]], base=0, channel_multiplier=0,
                      allow_small_or_imprecise_dtypes=True).then_inc(consts, 1)
            pool.iota(iota_r[:], pattern=[[1, CAP]], base=0, channel_multiplier=0,
                      allow_small_or_imprecise_dtypes=True).then_inc(consts, 1)
            pool.iota(idv[:].rearrange("p t k -> p (t k)"), pattern=[[P, NT], [T, 2]], base=1, channel_multiplier=1,
                      allow_small_or_imprecise_dtypes=True).then_inc(consts, 1)
            pool.iota(thr[:], pattern=[[CAP, MAXPASS]], base=0, channel_multiplier=0,
                      allow_small_or_imprecise_dtypes=True).then_inc(consts, 1)
            pool.wait_ge(ms_ready, 1)
            pool.tensor_tensor(rst[:], msq[:], mhalf[:], ALU.pow).then_inc(rms_ready, 1)
            pool.wait_ge(rms_copied, 1)
            pool.wait_ge(gmix_applied, 1)
            for c in range(1, NC, 2):
                pool.tensor_tensor(h_raw[:, c, :], h_raw[:, c, :], rms_all, ALU.mult).then_inc(h_ready[1], 1)
            with pool.Fori(0, NJ) as j:
                pool.wait_ge(var_eps, j + 1)
                pool.tensor_tensor(lnr[:], lnv[:], mhalf[:], ALU.pow).then_inc(ln_rstd, 1)
            for t in range(NT):
                pool.wait_ge(msq_ready, t + 1)
                pool.tensor_tensor(rst[:, t:t + 1], msq[:, t:t + 1], mhalf[:, 0:1], ALU.pow).then_inc(rst_ready, 1)
            pool.wait_ge(o_done, 2 * NT)
            for s in range(2):
                pool.memset(xg[s], 0.0).then_inc(xg_clear, 1)
            pool.wait_ge(xg_clear, 2)
            pool.wait_ge(h2_stored, 16 * NT)

            def gather(b, n, i, s):
                n_1, freed = pool.to_reg(n + 1), pool.to_reg(i + 1)
                pool.wait_ge(np_ready, 1)
                pool.wait_ge(xT_done[s], freed)
                pool.tensor_copy(gat_idx[:, s:s + 1], tok_tab[:, bass.ds(b, 1)] if not isinstance(b, int)
                                 else tok_tab[:, b:b + 1]).then_inc(gidx_copied, 1)
                pool.wait_ge(h2_stored, 16 * NT)
                pool.wait_ge(gidx_copied, n_1)
                pool.indirect_dma_start(xg[s], None, h2_dram,
                                        bass.IndirectOffsetOnAxis(ap=gat_idx[:, s:s + 1], axis=0),
                                        bounds_check=T - 1, oob_is_err=False).then_inc(gathered[s], 16)

            def scatter(b, n, i, s):
                n_1, n_2 = pool.to_reg(n + 1), pool.to_reg(n + 2)
                pool.tensor_copy(sca_idx[:, s:s + 1], id_tab[:, bass.ds(b, 1)] if not isinstance(b, int)
                                 else id_tab[:, b:b + 1]).then_inc(sidx_copied, 1)
                pool.wait_ge(np_ready, 1)
                pool.wait_ge(sidx_copied, n_1)
                for h in range(2):
                    pool.wait_ge(ye_ready[h], n_2)
                pool.indirect_dma_start(y_dram, bass.IndirectOffsetOnAxis(ap=sca_idx[:, s:s + 1], axis=0), ye[s],
                                        None, bounds_check=2 * T - 1, oob_is_err=False).then_inc(scattered[s], 16)

            def free_rows(i, s):
                landed = pool.to_reg(16 * i + 16)
                pool.wait_ge(np_ready, 1)
                pool.wait_ge(scattered[s], landed)
                pool.sem_inc(ye_free[s], 1)

            n_pass = passes(pool)
            with pool.Fori(0, n_pass) as p:
                n0, i0 = NE * p, (NE // 2) * p
                tables = pool.to_reg(2 * p + 2)
                pool.wait_ge(np_ready, 1)
                pool.wait_ge(tab_ready, tables)
                for k in range(5):
                    gather(k, n0 + k, i0 + k // 2, k % 2)
                scatter(0, n0, i0, 0)
                with pool.Fori(0, NE // 2 - 3) as i:
                    gather(2 * i + 5, n0 + 2 * i + 5, i0 + i + 2, 1)
                    scatter(2 * i + 1, n0 + 2 * i + 1, i0 + i, 1)
                    free_rows(i0 + i, 0)
                    gather(2 * i + 6, n0 + 2 * i + 6, i0 + i + 3, 0)
                    scatter(2 * i + 2, n0 + 2 * i + 2, i0 + i + 1, 0)
                    free_rows(i0 + i, 1)
                gather(NE - 1, n0 + NE - 1, i0 + NE // 2 - 1, 1)
                for k in range(NE - 5, NE):
                    scatter(k, n0 + k, i0 + k // 2, k % 2)
                    free_rows(i0 + (k - 1) // 2, (k - 1) % 2)
                free_rows(i0 + NE // 2 - 1, 1)
                pool.sem_inc(pass_closed, 1)
            for t in range(NT):
                pool.wait_ge(fms, t + 1)
                pool.tensor_tensor(rst[:, t:t + 1], msq[:, t:t + 1], mhalf[:, 0:1], ALU.pow).then_inc(frs, 1)

        @block.tensor
        def _(pe):
            for s_ in (vT_done, z_done, *xT_done, *unit_used, hidT_ps, *down_done):
                pe.sem_inc(s_, 1)
            pe.wait_ge(consts, 9)
            pe.wait_ge(squares_summed, NC - 1)
            for n in range(NT):
                last = pe.matmul(bank[4][:, n:n + 1], sq_sum[:, n * P:(n + 1) * P], ones[:, 0:1], start=True, stop=True)
            last.then_inc(ms_summed, 1)
            for n in range(NT):
                pe.wait_ge(diag_ready, n + 1)
                last = pe.matmul(bank[3][:, n * P:(n + 1) * P], ones[:], rms_diag[:, n, :], start=True, stop=True)
            last.then_inc(rms_spread, 1)

            def project(j, k, first=False):
                pe.wait_ge(in_lo_done, KINDS * j + k + 1)
                for c in range(NC):
                    if first:
                        pe.wait_ge(h_lo_done, c + 1)
                    for w, h in ((in_hi, h_hi), (in_hi, h_lo), (in_lo, h_hi)):
                        last = pe.matmul(bank[k], w[k][:, c * P:(c + 1) * P], h[:, c, :],
                                         start=(c == 0 and w is in_hi and h is h_hi),
                                         stop=(c == NC - 1 and w is in_lo))
                last.then_inc(proj_done, 1)

            def mix_pe(j, first=False):
                pe.wait_ge(zb_done, j + 1)
                project(j, V_, first)
                pe.wait_ge(u_gelu, j + 1)
                project(j, U_)
                pe.wait_ge(v_gelu, j + 1)
                pe.wait_ge(vhat_ready, j + 1)
                for n in range(NT):
                    last = pe.transpose(bank[7][:, n * P:(n + 1) * P], g_v[:, n * P:(n + 1) * P], ident[:])
                last.then_inc(vT_done, 1)
                pe.wait_ge(cc_copied, j + 1)
                project(j, CC_)
                pe.wait_ge(vhat_ready, j + 2)
                for n in range(NT):
                    w_sp_j = (w_sp[:, j, :] if isinstance(j, int)
                              else w_sp[:, bass.ds(j, 1), :].rearrange("p o q -> p (o q)"))
                    last = pe.matmul(bank[0][:, n * P:(n + 1) * P], vhat[:, n * P:(n + 1) * P], w_sp_j,
                                     start=True, stop=True)
                last.then_inc(z_done, 1)
                for k, free in ((XC_, conv_in), (CB_, yb_done), (GB_, tanh_b), (GA_, tanh_a)):
                    pe.wait_ge(free, j + 1)
                    project(j, k)

            mix_pe(0, first=True)
            with pe.Fori(1, NJ) as j:
                mix_pe(j)

            def out_proj(t, halves=(0, 1)):
                if t >= 2 and halves[0] == 0:
                    pe.wait_ge(x2_ready, 2 * (t - 2) + 2)
                order = [k for k in range(NC) if k != GA_] + [GA_]
                if t == 0:
                    steps = [(k, h) for k in order for h in range(2)]
                else:
                    steps = [(k, h) for h in halves for k in order]
                for k, h in steps:
                    if t == 0 and h == 0:
                        pe.wait_ge(in_lo_done, KINDS * NJ + (k + 1 if k < GA_ else k if k > GA_ else NC))
                        pe.wait_ge(m_lo_done, k + 1)
                    rows = slice(t * P, (t + 1) * P)
                    cols = slice(h * HALF, (h + 1) * HALF)
                    for i, (m, w) in enumerate(((m_hi[:, k, rows], in_hi[k]), (m_hi[:, k, rows], in_lo[k]),
                                                (m_lo[k][:, rows], in_hi[k]))):
                        last = pe.matmul(bank[2 * (t % 2) + h], m, w[:, cols], start=(k == order[0] and i == 0),
                                         stop=(k == order[-1] and i == 2))
                    if k == order[-1]:
                        last.then_inc(o_done, 1)

            def router(t):
                pe.wait_ge(h2_ready, t + 1)
                for h in range(2):
                    if t >= 1:
                        pe.wait_ge(h2T_ready, 2 * t - 1 + h)
                    for c in range(4):
                        last = pe.transpose(bank[4 + h][:, c * P:(c + 1) * P], h2p[:, t, 4 * h + c, :], ident[:])
                    last.then_inc(h2T_ps, 1)
                if t == 0:
                    pe.wait_ge(wr_in, 32)
                if t >= 1:
                    pe.wait_ge(logits_read, t)
                for c in range(NC):
                    if c % 4 == 0:
                        pe.wait_ge(h2T_ready, 2 * t + c // 4 + 1)
                    last = pe.matmul(bank[6][:, 0:NG + NE], h2T[:, c, :], wr[:, c, :], start=(c == 0), stop=(c == NC - 1))
                last.then_inc(logits, 1)

            def prefix(t):
                pe.wait_ge(member_ready, t + 1)
                for q in range(t + 1):
                    last = pe.matmul(bank[7][:, t * NE:(t + 1) * NE], upper[:] if q == t else ones[:], member[:, q, :],
                                     start=(q == 0), stop=(q == t))
                if t == NT - 1:
                    for q in range(NT):
                        last = pe.matmul(bank[7][:, NT * NE:(NT + 1) * NE], ones[:], member[:, q, :],
                                         start=(q == 0), stop=(q == NT - 1))
                last.then_inc(prefix_done, 1)

            pe.wait_ge(zb_done, NJ + 1)
            pe.wait_ge(u_gelu, NJ + 1)
            out_proj(0)
            out_proj(1)
            router(0)
            out_proj(2)
            prefix(0)
            router(1)
            out_proj(3, (0,))
            prefix(1)
            router(2)
            out_proj(3, (1,))
            prefix(2)
            router(3)
            prefix(3)

            def transpose_rows(i, s):
                landed = pe.to_reg(16 * i + 16)
                pe.wait_ge(consts, 9)
                pe.wait_ge(gathered[s], landed)
                for c in range(NC):
                    last = pe.transpose(bank[6][:, c * CAP:(c + 1) * CAP], xg[s][:, c * P:(c + 1) * P],
                                        ident[0:CAP, 0:CAP])
                last.then_inc(xT_done[s], 1)

            def product(n, s, half, b):
                for u in range(UNITS):
                    k = half * UNITS + u
                    pe.wait_ge(lo_done[k], n + 1)
                    for c in range(UC):
                        for part in (w_hi, w_lo):
                            last = pe.matmul(bank[b], xs[:, s, u * UC + c, :],
                                             part[:, k % RING, c * FE:(c + 1) * FE],
                                             start=(u == 0 and c == 0 and part is w_hi),
                                             stop=(u == UNITS - 1 and c == UC - 1 and part is w_lo))
                    last.then_inc(unit_used[k], 1)

            def hid_transposes(n):
                hid_n, copied = pe.to_reg(n + 2), pe.to_reg(n + 1)
                pe.wait_ge(consts, 9)
                pe.wait_ge(hid_ready, hid_n)
                pe.wait_ge(hidT_ready, copied)
                for c in range(NF):
                    last = pe.transpose(bank[7][:, c * CAP:(c + 1) * CAP], hid[:, c * P:(c + 1) * P],
                                        ident[0:CAP, 0:CAP])
                last.then_inc(hidT_ps, 1)

            def down(n, i, s):
                pe.wait_ge(hidT_ready, n + 2)
                for h in range(2):
                    pe.wait_ge(ye_ready[h], n + 1)
                for c in range(NF):
                    if c % (NF // 2) == 0:
                        pe.wait_ge(dn_in[2 * s + c // (NF // 2)], 16 * i + 16)
                    for h in range(2):
                        last = pe.matmul(bank[4 + h][0:CAP, :], hidT[:, c, :],
                                         dn_raw[:, s, c * D + h * HALF:c * D + (h + 1) * HALF],
                                         start=(c == 0), stop=(c == NF - 1))
                        if c == NF - 1:
                            last.then_inc(down_done[h], 1)

            def pe_block(n, i, s, has_prev, has_next, i_prev, i_next):
                pe.wait_ge(xlo_done, n + 2)
                pe.wait_ge(g_summed[s], i + 1)
                product(n, s, 0, s)
                if has_next:
                    transpose_rows(i_next, 1 - s)
                if has_prev:
                    hid_transposes(n - 1)
                pe.wait_ge(u_summed[s], i + 1)
                product(n, s, 1, 2 + s)
                if has_prev:
                    down(n - 1, i_prev, 1 - s)

            n_pass = passes(pe)
            with pe.Fori(0, n_pass) as p:
                n0, i0 = NE * p, (NE // 2) * p
                pe.wait_ge(rv_ready, 2 * NT * p + 2 * NT)
                for q in range(2 * NT):
                    last = pe.matmul(bank[7][0:CAP, 0:NE], r_all[:, q, :], v_all[:, q, :], start=(q == 0),
                                     stop=(q == 2 * NT - 1))
                last.then_inc(tab_ps, 1)
                pe.wait_ge(xlo_done, n0 + 1)
                transpose_rows(i0, 0)
                pe.wait_ge(tab_ready, 2 * p + 2)
                pe_block(n0, i0, 0, False, True, None, i0)
                with pe.Fori(0, NE // 2 - 1) as i:
                    pe_block(n0 + 2 * i + 1, i0 + i, 1, True, True, i0 + i, i0 + i + 1)
                    pe_block(n0 + 2 * i + 2, i0 + i + 1, 0, True, True, i0 + i, i0 + i + 1)
                pe_block(n0 + NE - 1, i0 + NE // 2 - 1, 1, True, False, i0 + NE // 2 - 1, None)
                hid_transposes(n0 + NE - 1)
                down(n0 + NE - 1, i0 + NE // 2 - 1, 1)

        @block.scalar
        def _(act):
            for s_ in (u_gelu, cc_copied, tanh_b, tanh_a, hidT_ready, g_act_ready, ye_ready[0]):
                act.sem_inc(s_, 1)
            def in_hi_copy(j, k):
                act.wait_ge(w_in_in[k], 16 * j + 16)
                act.activation(in_hi[k], in_raw[k], ACT.Copy).then_inc(in_hi_done, 1)

            for c in range(NC):
                act.wait_ge(xT_in[c // 2], 16)
                act.activation(squares[c], h_raw[:, c, :], ACT.Square).then_inc(squared, 1)
            in_hi_copy(0, V_)
            act.wait_ge(gmix_in, 16)
            act.wait_ge(squared, NC)
            for c in range(1, NC, 2):
                last = act.activation(h_raw[:, c, :], h_raw[:, c, :], ACT.Copy, scale=gmix[:, c:c + 1])
            last.then_inc(gmix_applied, 1)
            act.wait_ge(rms_spread, 1)
            act.activation(rms_all, bank[3], ACT.Copy).then_inc(rms_copied, 1)
            for c in range(NC):
                act.wait_ge(h_ready[c % 2], c // 2 + 1)
                act.activation(h_hi[:, c, :], h_raw[:, c, :], ACT.Copy).then_inc(h_hi_done, 1)
            for k in range(U_, GA_):
                in_hi_copy(0, k)

            def mix_act(j):
                in_hi_copy(j, GA_)
                act.wait_ge(proj_done, KINDS * j + V_ + 1)
                act.wait_ge(vT_done, j + 1)
                act.activation(g_v, bank[0], ACT.Gelu_apprx_tanh).then_inc(v_gelu, 1)
                act.wait_ge(merged_done, j + 1)
                act.wait_ge(proj_done, KINDS * j + U_ + 1)
                act.activation(g_u, bank[1], ACT.Gelu_apprx_tanh).then_inc(u_gelu, 1)
                in_hi_copy(j + 1, V_)
                act.wait_ge(proj_done, KINDS * j + CC_ + 1)
                act.activation(c_c, bank[2], ACT.Copy).then_inc(cc_copied, 1)
                for k in (U_, CC_, XC_):
                    in_hi_copy(j + 1, k)
                act.wait_ge(proj_done, KINDS * j + GB_ + 1)
                act.activation(t_b, bank[5], ACT.Tanh, scale=0.5).then_inc(tanh_b, 1)
                in_hi_copy(j + 1, CB_)
                act.wait_ge(proj_done, KINDS * j + GA_ + 1)
                act.activation(t_a, bank[6], ACT.Tanh, scale=0.5).then_inc(tanh_a, 1)
                in_hi_copy(j + 1, GB_)
                act.wait_ge(merged_done, j + 2)
                act.activation(m_hi[:, bass.ds(j, 1), :].rearrange("p o t -> p (o t)"), cnv, ACT.Copy
                               ).then_inc(m_hi_done, 1)

            with act.Fori(0, NJ) as j:
                mix_act(j)
            act.wait_ge(w_in_in[KINDS], 16)
            act.activation(in_hi[KINDS], in_raw[KINDS], ACT.Copy).then_inc(in_hi_done, 1)
            in_hi_copy(NJ, GA_)

            def act_square(t):
                act.wait_ge(x2_ready, 2 * t + 2)
                if t >= 1:
                    act.wait_ge(ssq_ready, t)
                act.activation(sq_dump, resid[:, t, :], ACT.Square, accum_out=ssq[:, t:t + 1]
                               ).then_inc(ssq_ready, 1)

            def act_router(t):
                for h in range(2):
                    act.wait_ge(h2T_ps, 2 * t + h + 1)
                    if t >= 1 and h == 0:
                        act.wait_ge(logits, t)
                    act.activation(h2T[:, 4 * h:4 * h + 4, :].rearrange("p c q -> p (c q)"),
                                   bank[4 + h], ACT.Copy).then_inc(h2T_ready, 1)
                act.wait_ge(ngm_ready, t + 1)
                act.activation(gexp[:], lg[:, 0:NG], ACT.Exp, bias=ngm[:], accum_out=gsum_e[:]).then_inc(gexp_done, 1)
                act.wait_ge(e2_ready, t + 1)
                act.activation(e2[:], eif[:, 0:1], ACT.Exp).then_inc(e2_done, 1)

            act_square(0)
            act_square(1)
            act_router(0)
            act_square(2)
            act_router(1)
            act_router(2)
            act_square(3)
            act_router(3)

            def hi_unit(n, i, s, half, u):
                k = half * UNITS + u
                if u == 0:
                    act.wait_ge(gu_in[2 * s + half], 16 * i + 16)
                if k >= RING:
                    act.wait_ge(unit_used[k - RING], n + 2)
                else:
                    act.wait_ge(unit_used[k + RING], n + 1)
                act.activation(w_hi[:, k % RING, :], gu_raw[:, 2 * s + half, u * UC * FE:(u + 1) * UC * FE],
                               ACT.Copy).then_inc(hi_done[k], 1)

            def x_hi(n, i, s):
                act.wait_ge(xT_done[s], i + 2)
                act.activation(xs[:, s, :, 0:CAP], bank[6].rearrange("p (c r) -> p c r", c=NC), ACT.Copy
                               ).then_inc(xhi_done, 1)

            def hid_copy(n):
                act.wait_ge(hidT_ps, n + 2)
                act.wait_ge(down_done[1], n + 1)
                act.activation(hidT[:, :, :].rearrange("p c r -> p (c r)"), bank[7][:, 0:NF * CAP], ACT.Copy
                               ).then_inc(hidT_ready, 1)

            def y_half(n, i, s):
                act.wait_ge(down_done[0], n + 2)
                act.wait_ge(ye_free[s], i + 1)
                act.activation(ye[s][:, 0:HALF], bank[4][0:CAP, :], ACT.Copy).then_inc(ye_ready[0], 1)

            def act_block(n, i, s, has_prev, has_next, i_prev, i_next):
                for u in range(UNITS):
                    hi_unit(n, i, s, 1, u)
                act.wait_ge(unit_used[UNITS - 1], n + 2)
                if has_prev:
                    act.wait_ge(g_summed[1 - s], i_prev + 2)
                act.activation(g_low, bank[s][CAP:2 * CAP, :], ACT.Copy).then_inc(g_low_ready, 1)
                if has_next:
                    x_hi(n + 1, i_next, 1 - s)
                if has_prev:
                    hid_copy(n - 1)
                if has_next:
                    hi_unit(n + 1, i_next, 1 - s, 0, 0)
                act.wait_ge(g_summed[s], i + 2)
                act.wait_ge(hid_ready, n + 1)
                act.activation(g_act, g_sum, ACT.Silu).then_inc(g_act_ready, 1)
                if has_next:
                    for u in range(1, UNITS):
                        hi_unit(n + 1, i_next, 1 - s, 0, u)
                act.wait_ge(unit_used[2 * UNITS - 1], n + 2)
                if has_prev:
                    act.wait_ge(u_summed[1 - s], i_prev + 2)
                act.activation(u_low, bank[2 + s][CAP:2 * CAP, :], ACT.Copy).then_inc(u_low_ready, 1)
                if has_prev:
                    y_half(n - 1, i_prev, 1 - s)

            n_pass = passes(act)
            with act.Fori(0, n_pass) as p:
                n0, i0 = NE * p, (NE // 2) * p
                for u in range(UNITS):
                    hi_unit(n0, i0, 0, 0, u)
                x_hi(n0, i0, 0)
                act_block(n0, i0, 0, False, True, None, i0)
                with act.Fori(0, NE // 2 - 1) as i:
                    act_block(n0 + 2 * i + 1, i0 + i, 1, True, True, i0 + i, i0 + i + 1)
                    act_block(n0 + 2 * i + 2, i0 + i + 1, 0, True, True, i0 + i, i0 + i + 1)
                act_block(n0 + NE - 1, i0 + NE // 2 - 1, 1, True, False, i0 + NE // 2 - 1, None)
                hid_copy(n0 + NE - 1)
                y_half(n0 + NE - 1, i0 + NE // 2 - 1, 1)

            for t in range(NT):
                act.wait_ge(comb1, t + 1)
                if t >= 1:
                    act.wait_ge(fsq, t)
                act.activation(sq_dump, resid[:, t, :], ACT.Square, accum_out=ssq[:, t:t + 1]).then_inc(fsq, 1)

        @block.vector
        def _(dve):
            for s_ in (zb_done, vhat_ready, conv_in, yb_done, merged_done, xlo_done, *g_summed, *u_summed, hid_ready, ye_ready[1]):
                dve.sem_inc(s_, 1)
            for c in range(1, NC):
                dve.wait_ge(squared, c + 1)
                if c >= 2:
                    dve.wait_ge(squares_summed, c - 1)
                dve.tensor_tensor(sq_sum, sq_sum, squares[c], ALU.add).then_inc(squares_summed, 1)
            dve.wait_ge(ms_summed, 1)
            dve.tensor_scalar(msq[:], bank[4][:, 0:NT], 1.0 / D, EPS, ALU.mult, ALU.add).then_inc(ms_ready, 1)
            dve.wait_ge(rms_ready, 1)
            for n in range(NT):
                dve.tensor_scalar(rms_diag[:, n, :], ident[:], rst[:, n:n + 1], None, ALU.mult
                                  ).then_inc(diag_ready, 1)

            def in_lo_sub(j, k):
                dve.wait_ge(in_hi_done, KINDS * j + k + 1)
                dve.tensor_tensor(in_lo[k], in_raw[k], in_hi[k].bitcast(F32), ALU.subtract
                                  ).then_inc(in_lo_done, 1)

            in_lo_sub(0, V_)
            dve.wait_ge(rms_copied, 1)
            dve.wait_ge(gmix_in, 16)

            def h_low(c):
                dve.wait_ge(h_hi_done, c + 1)
                dve.tensor_tensor(h_lo[:, c, :], h_raw[:, c, :], h_hi[:, c, :].bitcast(F32), ALU.subtract
                                  ).then_inc(h_lo_done, 1)

            for c in range(0, NC, 2):
                dve.scalar_tensor_tensor(h_raw[:, c, :], h_raw[:, c, :], gmix[:, c:c + 1], rms_all, ALU.mult,
                                         ALU.mult).then_inc(h_ready[0], 1)
                if c >= 2:
                    h_low(c - 2)
                    h_low(c - 1)
            h_low(NC - 2)
            h_low(NC - 1)
            for k in range(U_, GA_):
                in_lo_sub(0, k)
            dve.wait_ge(small_in, 64)

            def mix_dve(j, j0, m_lo_half):
                dve.tensor_copy(par[:, 0:3], wconv[:, bass.ds(j, 1), :].rearrange("p o k -> p (o k)")
                                ).then_inc(par_ready, 1)
                dve.tensor_copy(par[:, 3:4], gsgu[:, bass.ds(j, 1)]).then_inc(par_ready, 1)
                in_lo_sub(j, GA_)
                dve.wait_ge(vT_done, j + 2)
                for n in range(NT):
                    last = dve.bn_stats(bnst[:, n, :], bank[7][:, n * P:(n + 1) * P])
                last.then_inc(stats, 1)
                stats_j = dve.to_reg(j + 1)
                dve.wait_ge(consts, 9)
                dve.wait_ge(stats, stats_j)
                for n in range(NT):
                    last = dve.bn_aggr(bnmv[:, n, :], bnst[:, n, :])
                last.then_inc(aggr, 1)
                dve.wait_ge(aggr, j + 1)
                dve.tensor_scalar(lnv[:], bnmv[:, :, 1], EPS, None, ALU.add).then_inc(var_eps, 1)
                dve.wait_ge(ln_rstd, j + 1)
                dve.wait_ge(z_done, j + 1)
                for n in range(NT):
                    last = dve.tensor_scalar(vhat[:, n * P:(n + 1) * P], bank[7][:, n * P:(n + 1) * P],
                                             bnmv[:, n, 0:1], lnr[:, n:n + 1], ALU.subtract, ALU.mult)
                last.then_inc(vhat_ready, 1)
                in_lo_sub(j + 1, V_)
                dve.wait_ge(z_done, j + 2)
                dve.wait_ge(par_ready, 2 * j + 2)
                for n in range(NT):
                    last = dve.scalar_tensor_tensor(a_z[:, n * P:(n + 1) * P], bank[0][:, n * P:(n + 1) * P],
                                                    par[:, 3:4],
                                                    b_sp[:, bass.ds(j, 1), :].rearrange("p o q -> p (o q)"),
                                                    ALU.mult, ALU.add)
                last.then_inc(zb_done, 1)
                dve.wait_ge(zb_done, j + 2)
                dve.wait_ge(u_gelu, j + 2)
                dve.tensor_tensor(a_z, a_z, g_u, ALU.mult).then_inc(az_done, 1)
                in_lo_sub(j + 1, U_)
                dve.wait_ge(cc_copied, j + 2)
                dve.wait_ge(proj_done, KINDS * j + XC_ + 1)
                dve.tensor_tensor(zc[:, 1:T + 1], bank[3], c_c, ALU.mult).then_inc(conv_in, 1)
                dve.wait_ge(conv_in, j + 2)
                dve.tensor_scalar(cnv, zc[:, 0:T], par[:, 0:1], None, ALU.mult).then_inc(conv0, 1)
                dve.wait_ge(conv0, j + 1)
                dve.scalar_tensor_tensor(cnv, zc[:, 1:T + 1], par[:, 1:2], cnv, ALU.mult, ALU.add).then_inc(conv1, 1)
                dve.wait_ge(conv1, j + 1)
                dve.scalar_tensor_tensor(cnv, zc[:, 2:T + 2], par[:, 2:3], cnv, ALU.mult, ALU.add).then_inc(conv2, 1)
                in_lo_sub(j + 1, CC_)
                dve.wait_ge(conv2, j + 1)
                dve.wait_ge(proj_done, KINDS * j + CB_ + 1)
                dve.tensor_tensor(cnv, bank[4], cnv, ALU.mult).then_inc(yb_done, 1)
                in_lo_sub(j + 1, XC_)
                dve.wait_ge(yb_done, j + 2)
                dve.wait_ge(tanh_b, j + 2)
                dve.scalar_tensor_tensor(cnv, t_b, 1.0, cnv, ALU.add, ALU.mult).then_inc(b_gated, 1)
                in_lo_sub(j + 1, CB_)
                dve.wait_ge(az_done, j + 1)
                dve.wait_ge(tanh_a, j + 2)
                dve.scalar_tensor_tensor(a_z, t_a, 1.0, a_z, ALU.add, ALU.mult).then_inc(a_gated, 1)
                dve.wait_ge(b_gated, j + 1)
                dve.wait_ge(a_gated, j + 1)
                dve.tensor_tensor(cnv, a_z, cnv, ALU.add).then_inc(merged_done, 1)
                in_lo_sub(j + 1, GB_)
                dve.wait_ge(m_hi_done, j + 1)
                dve.tensor_tensor(m_lo_half[:, bass.ds(j - j0, 1), :].rearrange("p o t -> p (o t)"), cnv,
                                  m_hi[:, bass.ds(j, 1), :].bitcast(F32).rearrange("p o t -> p (o t)"), ALU.subtract
                                  ).then_inc(m_lo_done, 1)

            with dve.Fori(0, NJ // 2) as j:
                mix_dve(j, 0, m_lo_a)
            with dve.Fori(NJ // 2, NJ) as j:
                mix_dve(j, NJ // 2, m_lo_b)
            dve.wait_ge(in_hi_done, KINDS * NJ + KINDS)
            dve.tensor_tensor(in_lo[KINDS], in_raw[KINDS], in_hi[KINDS].bitcast(F32), ALU.subtract
                              ).then_inc(in_lo_done, 1)
            dve.wait_ge(in_hi_done, KINDS * NJ + NC)
            dve.tensor_tensor(in_lo[GA_], in_raw[GA_], in_hi[GA_].bitcast(F32), ALU.subtract).then_inc(in_lo_done, 1)

            step = [0]

            def link(ins):
                step[0] += 1
                ins.then_inc(rstep, 1)
                dve.wait_ge(rstep, step[0])

            def residual(t):
                if t == 0:
                    dve.wait_ge(x_in, 16)
                for h in range(2):
                    dve.wait_ge(o_done, 2 * t + h + 1)
                    dve.scalar_tensor_tensor(resid[:, t, h * HALF:(h + 1) * HALF], bank[2 * (t % 2) + h], 0.5,
                                             resid[:, t, h * HALF:(h + 1) * HALF], ALU.mult, ALU.add
                                             ).then_inc(x2_ready, 1)
                dve.wait_ge(ssq_ready, t + 1)
                dve.tensor_scalar(msq[:, t:t + 1], ssq[:, t:t + 1], 1.0 / D, EPS, ALU.mult, ALU.add
                                  ).then_inc(msq_ready, 1)
                dve.wait_ge(gffn_in, 16)
                dve.wait_ge(rst_ready, t + 1)
                dve.scalar_tensor_tensor(h2p[:, t, :, :].rearrange("p c q -> p q c"),
                                         resid[:, t, :].rearrange("p (q c) -> p q c", c=NC), rst[:, t:t + 1],
                                         gffn.rearrange("p (q c) -> p q c", c=NC), ALU.mult, ALU.mult
                                         ).then_inc(h2_ready, 1)

            def rank_onehot(t):
                for k in range(2):
                    dve.tensor_scalar(r_all[:, 2 * t + k, :], iota_r[:], rank[:, t, k:k + 1], None, ALU.is_equal
                                      ).then_inc(rv_ready, 1)

            def route(t):
                dve.wait_ge(logits, t + 1)
                if t >= 1:
                    dve.wait_ge(e2_done, t)
                dve.tensor_copy(lg[:], bank[6][:, 0:NG + NE]).then_inc(logits_read, 1)
                dve.wait_ge(logits_read, t + 1)
                link(dve.max(gmax[:], lg[:, 0:NG]))
                dve.tensor_scalar(ngm[:], gmax[:, 0:1], -1.0, None, ALU.mult).then_inc(ngm_ready, 1)
                link(dve.max_index(gidx[:], gmax[:], lg[:, 0:NG]))
                link(dve.tensor_copy(gidf[:], gidx[:, 0:1]))
                link(dve.tensor_scalar(gmask[:], iota_e[:, 0:NG], gidf[:], None, ALU.is_equal))
                link(dve.tensor_tensor(elm[:].rearrange("p (g e) -> p g e", g=NG),
                                       lg[:, NG:NG + NE].rearrange("p (g e) -> p g e", g=NG),
                                       gmask[:].unsqueeze(2).to_broadcast([P, NG, NE // NG]), ALU.mult))
                link(dve.tensor_reduce(el8[:], elm[:].rearrange("p (g e) -> p e g", g=NG), AX.X, ALU.add))
                link(dve.max(em8[:], el8[:]))
                link(dve.max_index(ei8[:], em8[:], el8[:]))
                link(dve.tensor_copy(eif[:], ei8[:, 0:2]))
                link(dve.scalar_tensor_tensor(eid[:, t, :], gidf[:].to_broadcast([P, 2]), float(NE // NG), eif[:],
                                              ALU.mult, ALU.add))
                for k in range(2):
                    link(dve.tensor_scalar(onehot[:, k, :], iota_e[:], eid[:, t, k:k + 1], None, ALU.is_equal))
                dve.tensor_tensor(member[:, t, :], onehot[:, 0, :], onehot[:, 1, :], ALU.add
                                  ).then_inc(member_ready, 1)
                dve.tensor_tensor(eif[:, 0:1], em8[:, 1:2], em8[:, 0:1], ALU.subtract).then_inc(e2_ready, 1)
                for k in range(2):
                    link(dve.tensor_scalar(v_all[:, 2 * t + k, :], iota_e[:], eid[:, t, k:k + 1], idv[:, t, k:k + 1],
                                           ALU.is_equal, ALU.mult))
                dve.wait_ge(gexp_done, t + 1)
                dve.wait_ge(e2_done, t + 1)
                link(dve.tensor_scalar(den[:], e2[:], 1.0, gsum_e[:], ALU.add, ALU.mult))
                link(dve.reciprocal(gate_w[:, t, 0:1], den[:]))
                dve.wait_ge(prefix_done, t + 1)
                if t == NT - 1:
                    link(dve.tensor_reduce(cmax[:], bank[7][:, NT * NE:(NT + 1) * NE], AX.X, ALU.max))
                    link(dve.tensor_scalar(thrm[:], thr[:], cmax[:], None, ALU.is_lt))
                    link(dve.tensor_reduce(npf[:], thrm[:], AX.X, ALU.add))
                    dve.tensor_copy(npi[:], npf[:]).then_inc(np_ready, 1)
                link(dve.tensor_tensor(gate_w[:, t, 1:2], gate_w[:, t, 0:1], e2[:], ALU.mult))
                for k in range(2):
                    link(dve.tensor_tensor_reduce(scratch[:], bank[7][:, t * NE:(t + 1) * NE], onehot[:, k, :],
                                                  1.0, 0.0, ALU.mult, ALU.add, rank[:, t, k:k + 1]))
                rank_onehot(t)

            residual(0)
            residual(1)
            route(0)
            residual(2)
            route(1)
            route(2)
            residual(3)
            route(3)

            def lo_unit(n, i, s, half, u):
                k = half * UNITS + u
                dve.wait_ge(hi_done[k], n + 1)
                dve.tensor_tensor(w_lo[:, k % RING, :], gu_raw[:, 2 * s + half, u * UC * FE:(u + 1) * UC * FE],
                                  w_hi[:, k % RING, :].bitcast(F32), ALU.subtract).then_inc(lo_done[k], 1)

            def x_lo(n, s):
                dve.wait_ge(xhi_done, n + 1)
                dve.tensor_tensor(xs[:, s, :, CAP:2 * CAP], bank[6].rearrange("p (c r) -> p c r", c=NC),
                                  xs[:, s, :, 0:CAP].bitcast(F32), ALU.subtract).then_inc(xlo_done, 1)

            def y_half(n, i, s):
                dve.wait_ge(down_done[1], n + 2)
                dve.wait_ge(ye_free[s], i + 1)
                dve.tensor_copy(ye[s][:, HALF:D], bank[5][0:CAP, :]).then_inc(ye_ready[1], 1)

            def dve_block(n, i, s, has_prev, has_next, i_prev, i_next):
                for u in range(UNITS):
                    lo_unit(n, i, s, 1, u)
                dve.wait_ge(g_low_ready, n + 1)
                dve.wait_ge(g_act_ready, n + 1)
                dve.tensor_tensor(g_sum, bank[s][0:CAP, :], g_low, ALU.add).then_inc(g_summed[s], 1)
                if has_next:
                    x_lo(n + 1, 1 - s)
                    for u in range(UNITS):
                        lo_unit(n + 1, i_next, 1 - s, 0, u)
                dve.wait_ge(u_low_ready, n + 1)
                dve.tensor_tensor(u_sum, bank[2 + s][0:CAP, :], u_low, ALU.add).then_inc(u_summed[s], 1)
                dve.wait_ge(u_summed[s], i + 2)
                dve.wait_ge(g_act_ready, n + 2)
                dve.wait_ge(hidT_ps, n + 1)
                dve.tensor_tensor(hid, u_sum, g_act, ALU.mult).then_inc(hid_ready, 1)
                if has_prev:
                    y_half(n - 1, i_prev, 1 - s)

            n_pass = passes(dve)
            with dve.Fori(0, n_pass) as p:
                n0, i0 = NE * p, (NE // 2) * p
                dve.wait_ge(rv_ready, 2 * NT * p + 2 * NT)
                dve.tensor_scalar(iota_r[:], iota_r[:], float(CAP), None, ALU.add).then_inc(tab_step, 1)
                dve.wait_ge(tab_ps, p + 1)
                dve.tensor_copy(tb_v[:], bank[7][0:CAP, 0:NE]).then_inc(tab_step, 1)
                dve.wait_ge(tab_step, 5 * p + 2)
                dve.tensor_scalar(tb_e[:], tb_v[:], 0.5, float(OUT_OF_RANGE), ALU.is_lt, ALU.mult).then_inc(tab_step, 1)
                dve.wait_ge(tab_step, 5 * p + 3)
                dve.scalar_tensor_tensor(tb_v[:], tb_v[:], -1.0, tb_e[:], ALU.add, ALU.add).then_inc(tab_step, 1)
                dve.wait_ge(tab_step, 5 * p + 4)
                dve.wait_ge(pass_closed, p + 1)
                dve.tensor_scalar(tb_e[:], tb_v[:], float(T) - 0.5, -float(T), ALU.is_gt, ALU.mult
                                  ).then_inc(tab_step, 1)
                dve.tensor_copy(id_tab[:], tb_v[:]).then_inc(tab_ready, 1)
                dve.wait_ge(tab_step, 5 * p + 5)
                dve.tensor_tensor(tok_tab[:], tb_v[:], tb_e[:], ALU.add).then_inc(tab_ready, 1)
                for u in range(UNITS):
                    lo_unit(n0, i0, 0, 0, u)
                x_lo(n0, 0)
                dve_block(n0, i0, 0, False, True, None, i0)
                with dve.Fori(0, NE // 2 - 1) as i:
                    dve_block(n0 + 2 * i + 1, i0 + i, 1, True, True, i0 + i, i0 + i + 1)
                    dve_block(n0 + 2 * i + 2, i0 + i + 1, 0, True, True, i0 + i, i0 + i + 1)
                dve_block(n0 + NE - 1, i0 + NE // 2 - 1, 1, True, False, i0 + NE // 2 - 1, None)
                y_half(n0 + NE - 1, i0 + NE // 2 - 1, 1)
                for t in range(NT):
                    rank_onehot(t)

            dve.wait_ge(gf_in, 16)

            def combine(t):
                dve.wait_ge(y_in[t], 16)
                dve.scalar_tensor_tensor(resid[:, t, :], gu_raw[:, t, 0:D], gate_w[:, t, 0:1], resid[:, t, :],
                                         ALU.mult, ALU.add).then_inc(comb0, 1)
                if t >= 1:
                    mean_square(t - 1)
                dve.wait_ge(comb0, t + 1)
                dve.scalar_tensor_tensor(resid[:, t, :], gu_raw[:, t, D:2 * D], gate_w[:, t, 1:2], resid[:, t, :],
                                         ALU.mult, ALU.add).then_inc(comb1, 1)

            def mean_square(t):
                dve.wait_ge(fsq, t + 1)
                dve.tensor_scalar(msq[:, t:t + 1], ssq[:, t:t + 1], 1.0 / D, EPS, ALU.mult, ALU.add).then_inc(fms, 1)

            def finish(t):
                dve.wait_ge(frs, t + 1)
                dve.scalar_tensor_tensor(dn_raw[:, 1, t * D:(t + 1) * D], resid[:, t, :], rst[:, t:t + 1], g_fin,
                                         ALU.mult, ALU.mult).then_inc(out_ready, 1)

            combine(0)
            for t in range(1, NT):
                combine(t)
                finish(t - 1)
            mean_square(NT - 1)
            finish(NT - 1)


_ORDER = (1, 0, 3, 4, 2, 6, 5)


def kernel(x, g_mix, w_in, w_s, b_s, g_sgu, w_conv, w_out, g_ffn, w_router_group, w_router_expert, w_gate, w_up,
           w_down, g_final):
    import numpy as np
    import concourse.bacc as bacc
    from concourse.bass_utils import run_bass_kernel_spmd

    x = np.asarray(x)
    arrays = {
        "xT": np.asarray(x)[0].T.reshape(P, NC, T),
        "x": x[0].reshape(NT, P, D).transpose(1, 0, 2),
        "g_mix": np.asarray(g_mix).reshape(P, NC),
        "w_in": np.asarray(w_in)[0].reshape(P, NC, KINDS, NJ, P)[:, :, list(_ORDER)].transpose(3, 0, 2, 1, 4)
                .reshape(NJ, P, KINDS, NC * P),
        "w_sT": np.asarray(w_s)[0].transpose(2, 0, 1),
        "b_s": np.asarray(b_s).reshape(NJ * P),
        "g_sgu": np.asarray(g_sgu).reshape(NJ, P).T,
        "w_conv": np.asarray(w_conv)[0].reshape(3, NJ, P).transpose(2, 1, 0),
        "w_out": np.asarray(w_out)[0].reshape(NC, P, D),
        "g_ffn": np.asarray(g_ffn).reshape(D),
        "w_rg": np.asarray(w_router_group)[0],
        "w_re": np.asarray(w_router_expert)[0],
        "w_gate": np.asarray(w_gate)[0],
        "w_up": np.asarray(w_up)[0],
        "w_down": np.asarray(w_down)[0],
        "g_final": np.asarray(g_final).reshape(D),
    }
    nc = bacc.Bacc("TRN2", target_bir_lowering=False, num_devices=1)
    feed, aps = {}, {}
    for name, a in arrays.items():
        feed["in_" + name] = np.ascontiguousarray(a)
        aps[name] = nc.dram_tensor("in_" + name, a.shape, F32, kind="ExternalInput").ap()
    h2_dram = nc.dram_tensor("h2_rows", (T, D), F32, kind="Internal").ap()
    y_dram = nc.dram_tensor("y_rows", (2 * T, D), F32, kind="Internal").ap()
    out = nc.dram_tensor("out_0", (T, D), F32, kind="ExternalOutput").ap()
    build(nc, **aps, h2_dram=h2_dram, y_dram=y_dram, out=out)
    r = run_bass_kernel_spmd(nc, [feed], core_ids=[0])
    return r.results[0]["out_0"].reshape(1, T, D)
```

```python
from contextlib import ExitStack

import concourse.bass as bass
from concourse import mybir

F32 = mybir.dt.float32
F32R = mybir.dt.float32r
I32 = mybir.dt.int32
U32 = mybir.dt.uint32
ALU = mybir.AluOpType
ACT = mybir.ActivationFunctionType
AX = mybir.AxisListType

P = 128
D = 1024
T = 512
NT = T // P
NC = D // P
NJ = D // P
KINDS = 7
V_, U_, CC_, XC_, CB_, GB_, GA_ = range(KINDS)
NG = 8
NE = 64
FE = 512
NF = FE // P
CAP = 64
SIZES = (CAP // 4, CAP // 2, CAP)
MAXPASS = T // CAP
UNITS = 4
UC = NC // UNITS
RING = 4
EPS = 1e-6
HALF = D // 2
OUT_OF_RANGE = 8192


def build(nc, xT, x, g_mix, w_in, w_sT, b_s, g_sgu, w_conv, w_out, g_ffn, w_rg, w_re, w_gate, w_up, w_down,
          g_final, h2_dram, y_dram, out):
    with ExitStack() as ctx:
        def sb(name, shape, dt=F32):
            return ctx.enter_context(nc.sbuf_tensor(name, shape, dt))

        def sem(name):
            return ctx.enter_context(nc.semaphore(name))

        def sb_both(name, shape):
            offset = -(-nc.sbuf_base // 32) * 32
            return sb(name, shape), nc.alloc_sbuf_tensor_at(name + "_r", shape, F32R, offset=offset)

        gu_raw, gu_raw_r = sb_both("gu_raw", [P, 4, NC * FE])
        dn_raw, dn_raw_r = sb_both("dn_raw", [P, 2, NF * D])
        arena, arena_r = sb_both("arena", [P, KINDS, NC * P])
        w_sp, w_sp_r = sb_both("w_sp", [P, NJ, P])
        b_sp, b_sp_r = sb_both("b_sp", [P, NJ, P])
        w_hi = sb("w_hi", [P, RING, UC * FE], F32R)
        w_lo_f, w_lo = sb_both("w_lo", [P, RING, UC * FE])
        xs = sb("xs", [P, 2, NC, 2 * CAP], F32R)
        resid = sb("resid", [P, NT, D])
        zc = sb("zc", [P, T + 2])
        m_lo_b = sb("m_lo_b", [P, NJ // 2, T], F32R)
        wr = sb("wr", [P, NC, NG + NE])
        ident = sb("ident", [P, P])
        ones = sb("ones", [P, P])
        upper = sb("upper", [P, P], F32R)
        ones_r = sb("ones_r", [P, P], F32R)
        iota_e = sb("iota_e", [P, NE])
        iota_r = sb("iota_r", [P, CAP])
        member = sb("member", [P, NT, NE], F32R)
        gmix = sb("gmix", [P, NC])
        gsgu = sb("gsgu", [P, NJ])
        wconv = sb("wconv", [P, NJ, 3])
        par = sb("par", [P, 4])
        mhalf = sb("mhalf", [P, NT])
        bnst = sb("bnst", [P, NT, 6])
        bnmv = sb("bnmv", [P, NT, 2])
        lnv = sb("lnv", [P, NT])
        lnr = sb("lnr", [P, NT])
        ssq = sb("ssq", [P, NT])
        msq = sb("msq", [P, NT])
        rst = sb("rst", [P, NT])
        gmax = sb("gmax", [P, 8])
        gidx = sb("gidx", [P, 8], U32)
        gidf = sb("gidf", [P, 1])
        ngm = sb("ngm", [P, 1])
        gexp = sb("gexp", [P, NG])
        gsum_e = sb("gsum_e", [P, 1])
        gmask = sb("gmask", [P, NG])
        lg = sb("lg", [P, NG + NE])
        elm = sb("elm", [P, NE])
        el8 = sb("el8", [P, 8])
        em8 = sb("em8", [P, 8])
        ei8 = sb("ei8", [P, 8], U32)
        eif = sb("eif", [P, 2])
        e2 = sb("e2", [P, 1])
        den = sb("den", [P, 1])
        eid = sb("eid", [P, NT, 2])
        onehot = sb("onehot", [P, 2, NE])
        rank = sb("rank", [P, NT, 2])
        gate_w = sb("gate_w", [P, NT, 2])
        idv = sb("idv", [P, NT, 2])
        cmax = sb("cmax", [P, 1])
        thr = sb("thr", [P, MAXPASS])
        thrm = sb("thrm", [P, MAXPASS])
        npf = sb("npf", [P, 1])
        npi = sb("npi", [P, 1], I32)
        tb_v = sb("tb_v", [CAP, NE])
        tb_e = sb("tb_e", [CAP, NE])
        tok_tab = sb("tok_tab", [CAP, NE], U32)
        id_tab = sb("id_tab", [CAP, NE], U32)
        total = sb("total", [1, NE])
        gat_idx = sb("gat_idx", [CAP, 2], U32)
        sca_idx = sb("sca_idx", [CAP, 2], U32)

        h_raw = gu_raw[:, 3, :].rearrange("p (c t) -> p c t", c=NC)
        h_lo = gu_raw_r[:, 2, :].rearrange("p (c t) -> p c t", c=NC)
        h_hi = dn_raw_r[:, 1, :].rearrange("p (c t) -> p c t", c=NC)
        h2p = dn_raw[:, 1, :].rearrange("p (t c q) -> p t c q", t=NT, c=NC)
        m_hi = gu_raw_r[:, 3, :].rearrange("p (k t) -> p k t", k=NJ)
        m_lo_a = xs[:, :, :, :].rearrange("p s c r -> p (s c r)").rearrange("p (k t) -> p k t", t=T)
        m_lo = [(m_lo_a if k < NJ // 2 else m_lo_b)[:, k % (NJ // 2), :] for k in range(NJ)]
        g_fin = gu_raw[:, 0, 2 * D:3 * D]
        h2T = gu_raw[:, 2, 0:D].rearrange("p (c q) -> p c q", c=NC)
        gffn = gu_raw[:, 2, D:2 * D]
        tmp = resid[:, :, :].rearrange("p a (b t) -> p (a b) t", b=2)
        g_v, g_u, c_c, t_b, t_a, cnv, a_z, vhat = (tmp[:, i, :] for i in range(8))
        squares = [tmp[:, c, :] for c in range(NC)]
        sq_sum = squares[0]
        rms_diag = tmp[:, 1, :].rearrange("p (n q) -> p n q", n=NT)
        rms_all, rms_sq = (w_lo_f[:, RING - 1, i * T:(i + 1) * T] for i in range(2))
        v_all = w_sp_r[:, 0:4, :].rearrange("p a (b e) -> p (a b) e", e=NE)
        r_all = w_sp_r[:, 4:8, :].rearrange("p a (b e) -> p (a b) e", e=CAP)
        work = arena[:, :, :].rearrange("p a b -> p (a b)")
        xg = [work[0:CAP, 0:D], work[0:CAP, D:2 * D]]
        ye = [work[0:CAP, 2 * D:3 * D], work[0:CAP, 3 * D:4 * D]]
        g_low, u_low, g_sum, u_sum, g_act, hid = (work[0:CAP, 4 * D + i * FE:4 * D + (i + 1) * FE] for i in range(6))
        hidT = b_sp[:, 0:2, :].rearrange("p a (b r) -> p (a b) r", r=CAP)
        sq_dump = zc[:, 0:T].bitcast(mybir.dt.bfloat16)
        in_hi = [w_hi[:, k, :] for k in range(RING)] + [w_lo[:, k, :] for k in range(RING)]
        in_raw = [arena[:, k, :] for k in range(KINDS)] + [b_sp[:, :, :].rearrange("p a b -> p (a b)")]
        in_lo = [arena_r[:, k, :] for k in range(KINDS)] + [b_sp_r[:, :, :].rearrange("p a b -> p (a b)")]

        over_1 = onehot[0:1, 0, :]
        size_f = onehot[0:1, 1, :]
        size_i = lg[0:1, 0:NE].bitcast(I32)

        bank = [ctx.enter_context(nc.psum_tensor(f"bank{i}", [P, 512], F32))[:, :] for i in range(4)]
        y_ps = ctx.enter_context(nc.psum_tensor("y_ps", [P, 1024], F32))
        bank += [y_ps[:, 0:512], y_ps[:, 512:1024]]
        bank += [ctx.enter_context(nc.psum_tensor(f"bank{i}", [P, 512], F32))[:, :] for i in (6, 7)]

        xT_in = [sem(f"xT_in{q}") for q in range(NC // 2)]
        gmix_in, small_in, wr_in, x_in = sem("gmix_in"), sem("small_in"), sem("wr_in"), sem("x_in")
        w_in_in = [sem(f"w_in_in{k}") for k in range(KINDS + 1)]
        gu_in = [sem(f"gu_in{k}") for k in range(4)]
        dn_in = [sem(f"dn_in{k}") for k in range(4)]
        consts = sem("consts")
        squared, squares_summed, ms_summed, ms_ready, rms_ready, diag_ready, rms_spread = (sem(n) for n in
            ("squared", "squares_summed", "ms_summed", "ms_ready", "rms_ready", "diag_ready", "rms_spread"))
        rms_squared = sem("rms_squared")
        v_scaled, u_scaled, cb_scaled, b_scaled, a_scaled = (sem(n) for n in
            ("v_scaled", "u_scaled", "cb_scaled", "b_scaled", "a_scaled"))
        rms_copied, h_hi_done, h_lo_done = sem("rms_copied"), sem("h_hi_done"), sem("h_lo_done")
        in_hi_done, in_lo_done = sem("in_hi_done"), sem("in_lo_done")
        proj_done, v_gelu, u_gelu, cc_scaled, tanh_b, tanh_a = (sem(n) for n in
            ("proj_done", "v_gelu", "u_gelu", "cc_scaled", "tanh_b", "tanh_a"))
        vT_done, z_done = sem("vT_done"), sem("z_done")
        par_ready, stats, aggr, var_eps, ln_rstd, vhat_ready = (sem(n) for n in
            ("par_ready", "stats", "aggr", "var_eps", "ln_rstd", "vhat_ready"))
        m_hi_done, m_lo_done, gffn_in, logits_read = (sem(n) for n in
            ("m_hi_done", "m_lo_done", "gffn_in", "logits_read"))
        conv_in, conv0, conv1, conv2, yb_done, zb_done, az_done, b_gated, a_gated, merged_done = (sem(n) for n in
            ("conv_in", "conv0", "conv1", "conv2", "yb_done", "zb_done", "az_done", "b_gated", "a_gated",
             "merged_done"))
        o_done, x2_ready, ssq_ready, msq_ready, rst_ready, h2_ready, h2_stored = (sem(n) for n in
            ("o_done", "x2_ready", "ssq_ready", "msq_ready", "rst_ready", "h2_ready", "h2_stored"))
        h2T_ps, h2T_ready, logits, gexp_done, e2_done, member_ready, prefix_done = (sem(n) for n in
            ("h2T_ps", "h2T_ready", "logits", "gexp_done", "e2_done", "member_ready", "prefix_done"))
        ngm_ready, e2_ready, rstep = sem("ngm_ready"), sem("e2_ready"), sem("rstep")
        np_ready, rv_ready, tab_ps, tab_step, tab_ready, xg_clear = (sem(n) for n in
            ("np_ready", "rv_ready", "tab_ps", "tab_step", "tab_ready", "xg_clear"))
        gidx_copied, sidx_copied = sem("gidx_copied"), sem("sidx_copied")
        gathered = [sem(f"gathered{s}") for s in range(2)]
        scattered = [sem(f"scattered{s}") for s in range(2)]
        xT_done = [sem(f"xT_done{s}") for s in range(2)]
        xhi_done, xlo_done = sem("xhi_done"), sem("xlo_done")
        hi_done = sem("hi_done")
        lo_done = [sem(f"lo_done{k}") for k in range(2 * UNITS)]
        unit_used = [sem(f"unit_used{k}") for k in range(2 * UNITS)]
        g_low_ready, u_low_ready, g_act_ready, hid_ready = (sem(n) for n in
            ("g_low_ready", "u_low_ready", "g_act_ready", "hid_ready"))
        g_summed = [sem(f"g_summed{s}") for s in range(2)]
        u_summed = [sem(f"u_summed{s}") for s in range(2)]
        hidT_ps, hidT_ready = sem("hidT_ps"), sem("hidT_ready")
        down_done = [sem(f"down_done{h}") for h in range(2)]
        ye_ready = [sem(f"ye_ready{h}") for h in range(2)]
        ye_free = [sem(f"ye_free{s}") for s in range(2)]
        pass_closed = sem("pass_closed")
        y_in = [sem(f"y_in{t}") for t in range(NT)]
        totals = sem("totals")
        gf_in, weights_ready = sem("gf_in"), sem("weights_ready")
        comb0, comb1, fsq, fms, frs, out_ready, out_stored = (sem(n) for n in
            ("comb0", "comb1", "fsq", "fms", "frs", "out_ready", "out_stored"))

        def passes(eng):
            eng.wait_ge(np_ready, 1)
            return eng.value_load(npi[0:1, 0:1], min_val=1, max_val=MAXPASS)

        block = ctx.enter_context(nc.Block())

        @block.sync
        def _(sp):
            sp.dma_start(arena[:, V_, :], w_in[0, :, V_, :]).then_inc(w_in_in[V_], 16)
            sp.dma_start(gmix[:], g_mix).then_inc(gmix_in, 16)
            for q in range(NC // 2):
                sp.dma_start(h_raw[:, 2 * q:2 * q + 2, :], xT[:, 2 * q:2 * q + 2, :]).then_inc(xT_in[q], 16)
            for k in range(U_, KINDS):
                sp.dma_start(arena[:, k, :], w_in[0, :, k, :]).then_inc(w_in_in[k], 16)
                if k == XC_:
                    sp.dma_start(gsgu[:], g_sgu).then_inc(small_in, 16)
                    sp.dma_start(wconv[:, :, :], w_conv).then_inc(small_in, 16)
                    sp.dma_start(w_sp[:, :, :], w_sT).then_inc(small_in, 16)
                    sp.dma_start(b_sp[:, :, :].rearrange("p g q -> p (g q)"), b_s.partition_broadcast(P)
                                 ).then_inc(small_in, 16)
            sp.dma_start(wr[:, :, 0:NG], w_rg.rearrange("(p c) g -> p c g", c=NC)).then_inc(wr_in, 16)
            sp.dma_start(wr[:, :, NG:NG + NE], w_re.rearrange("(p c) g -> p c g", c=NC)).then_inc(wr_in, 16)

            def load_gate_up(e, s, half):
                w = (w_gate, w_up)[half]
                sp.dma_start(gu_raw[:, 2 * s + half, :], w[bass.ds(e, 1)].rearrange("o (p c) f -> (o p) (c f)", c=NC)
                             if not isinstance(e, int) else w[e].rearrange("(p c) f -> p (c f)", c=NC)
                             ).then_inc(gu_in[2 * s + half], 16)

            def load_down(e, s):
                for half in range(2):
                    src = (w_down[bass.ds(e, 1)].rearrange("o (c p) d -> (o p) c d", p=P)
                           if not isinstance(e, int) else w_down[e].rearrange("(c p) d -> p c d", p=P))
                    cs = slice(half * NF // 2, (half + 1) * NF // 2)
                    sp.dma_start(dn_raw[:, s, :].rearrange("p (c d) -> p c d", c=NF)[:, cs, :], src[:, cs, :]
                                 ).then_inc(dn_in[2 * s + half], 16)

            def load_in(j, k):
                sp.wait_ge(proj_done, KINDS * j - KINDS + k + 1)
                sp.dma_start(arena[:, k, :], w_in[bass.ds(j, 1), :, k, :].rearrange("o p n -> (o p) n")
                             if not isinstance(j, int) else w_in[j, :, k, :]).then_inc(w_in_in[k], 16)

            for k in range(KINDS):
                load_in(1, k)
                if k == CC_:
                    load_gate_up(0, 0, 0)
                elif k == CB_:
                    load_gate_up(0, 0, 1)
                elif k == GA_:
                    load_down(0, 0)
            with sp.Fori(2, NJ) as j:
                for k in range(KINDS):
                    load_in(j, k)
            for k in range(KINDS):
                if k == XC_:
                    sp.wait_ge(zb_done, NJ + 1)
                    sp.dma_start(in_raw[NC - 1], w_out[NC - 1]).then_inc(w_in_in[KINDS], 16)
                sp.wait_ge(proj_done, KINDS * (NJ - 1) + k + 1)
                sp.dma_start(in_raw[k], w_out[k]).then_inc(w_in_in[k], 16)
            sp.dma_start(gffn, g_ffn.partition_broadcast(P)).then_inc(gffn_in, 16)
            sp.wait_ge(m_lo_done, NJ)
            sp.dma_start(resid[:, :, :], x).then_inc(x_in, 16)
            for t in range(NT):
                sp.wait_ge(h2_ready, t + 1)
                sp.dma_start(h2_dram[t * P:(t + 1) * P, :], h2p[:, t, :, :].rearrange("p c q -> p (c q)")
                             ).then_inc(h2_stored, 16)
            sp.wait_ge(o_done, 2 * NT)
            load_gate_up(1, 1, 1)
            sp.wait_ge(h2_stored, 16 * NT)
            sp.wait_ge(h2T_ps, 2 * NT)
            load_down(1, 1)
            sp.wait_ge(logits, NT)
            sp.wait_ge(gathered[0], 16)
            load_gate_up(1, 1, 0)

            def load_next_gate_up(e, n, s):
                sp.wait_ge(lo_done[UNITS - 1], n - 1)
                load_gate_up(e, s, 0)
                sp.wait_ge(lo_done[2 * UNITS - 1], n - 1)
                load_gate_up(e, s, 1)

            def load_next_down(e, n, s):
                sp.wait_ge(down_done[1], n)
                load_down(e, s)

            load_next_gate_up(2, 2, 0)
            load_next_gate_up(3, 3, 1)
            load_next_down(2, 2, 0)
            with sp.Fori(2, NE // 2) as i:
                for s in range(2):
                    n = 2 * i + s
                    load_next_gate_up(n, n, s)
                    load_next_down(n - 1, n - 1, 1 - s)
            load_next_down(NE - 1, NE - 1, 1)
            n_pass = passes(sp)
            with sp.If(n_pass > 1):
                with sp.Fori(1, n_pass) as p:
                    n0 = NE * p
                    load_next_gate_up(0, n0, 0)
                    load_next_gate_up(1, n0 + 1, 1)
                    load_next_down(0, n0, 0)
                    with sp.Fori(1, NE // 2) as i:
                        for s in range(2):
                            load_next_gate_up(2 * i + s, n0 + 2 * i + s, s)
                            load_next_down(2 * i + s - 1, n0 + 2 * i + s - 1, 1 - s)
                    load_next_down(NE - 1, n0 + NE - 1, 1)
            scatters, blocks = sp.to_reg(16 * (NE // 2) * n_pass), sp.to_reg(NE * n_pass)
            sp.wait_ge(np_ready, 1)
            sp.wait_ge(lo_done[2 * UNITS - 1], blocks)
            sp.dma_start(g_fin, g_final.partition_broadcast(P)).then_inc(gf_in, 16)
            sp.wait_ge(np_ready, 1)
            for s in range(2):
                sp.wait_ge(scattered[s], scatters)
            for t in range(NT):
                sp.dma_start(gu_raw[:, t, 0:2 * D].rearrange("p (k d) -> p k d", k=2),
                             y_dram.rearrange("(k t) d -> t k d", k=2)[t * P:(t + 1) * P]).then_inc(y_in[t], 16)
            for t in range(NT):
                sp.wait_ge(out_ready, t + 1)
                sp.dma_start(out[t * P:(t + 1) * P, :], dn_raw[:, 1, t * D:(t + 1) * D]).then_inc(out_stored, 16)
            sp.wait_ge(out_stored, 16 * NT)

        @block.gpsimd
        def _(pool):
            for s_ in (*ye_free, pass_closed):
                pool.sem_inc(s_, 1)
            pool.memset(ones[:], 1.0).then_inc(consts, 1)
            pool.memset(zc[:], 0.0).then_inc(consts, 1)
            pool.memset(mhalf[:], -0.5).then_inc(consts, 1)
            pool.wait_ge(consts, 3)
            pool.affine_select(ident[:], ones[:], pattern=[[-1, P]], compare_op=ALU.is_equal, fill=0.0, base=0,
                               channel_multiplier=1).then_inc(consts, 1)
            pool.tensor_scalar(ones_r[:], ones[:], 1.0, None, ALU.mult).then_inc(consts, 1)
            pool.affine_select(upper[:], ones[:], pattern=[[1, P]], compare_op=ALU.is_gt, fill=0.0, base=0,
                               channel_multiplier=-1).then_inc(consts, 1)
            pool.iota(iota_e[:], pattern=[[1, NE]], base=0, channel_multiplier=0,
                      allow_small_or_imprecise_dtypes=True).then_inc(consts, 1)
            pool.iota(iota_r[:], pattern=[[1, CAP]], base=0, channel_multiplier=0,
                      allow_small_or_imprecise_dtypes=True).then_inc(consts, 1)
            pool.iota(idv[:].rearrange("p t k -> p (t k)"), pattern=[[P, NT], [T, 2]], base=1, channel_multiplier=1,
                      allow_small_or_imprecise_dtypes=True).then_inc(consts, 1)
            pool.iota(thr[:], pattern=[[CAP, MAXPASS]], base=0, channel_multiplier=0,
                      allow_small_or_imprecise_dtypes=True).then_inc(consts, 1)
            pool.wait_ge(ms_ready, 1)
            pool.tensor_tensor(rst[:], msq[:], mhalf[:], ALU.pow).then_inc(rms_ready, 1)
            with pool.Fori(0, NJ) as j:
                pool.wait_ge(var_eps, j + 1)
                pool.tensor_tensor(lnr[:], lnv[:], mhalf[:], ALU.pow).then_inc(ln_rstd, 1)
            for t in range(NT):
                pool.wait_ge(msq_ready, t + 1)
                pool.tensor_tensor(rst[:, t:t + 1], msq[:, t:t + 1], mhalf[:, 0:1], ALU.pow).then_inc(rst_ready, 1)
            pool.wait_ge(o_done, 2 * NT)
            for s in range(2):
                pool.memset(xg[s], 0.0).then_inc(xg_clear, 1)
            pool.wait_ge(xg_clear, 2)
            pool.wait_ge(h2_stored, 16 * NT)

            def size_class(b):
                return pool.value_load(size_i[0:1, bass.ds(b, 1)] if not isinstance(b, int) else size_i[0:1, b:b + 1],
                                       min_val=0, max_val=2)

            def by_size(size, move, s):
                with pool.If(size > 1):
                    move(s, SIZES[2])
                with pool.Else():
                    with pool.If(size > 0):
                        move(s, SIZES[1])
                    with pool.Else():
                        move(s, SIZES[0])

            def gather_rows(s, rows):
                pool.indirect_dma_start(xg[s][0:rows, :], None, h2_dram,
                                        bass.IndirectOffsetOnAxis(ap=gat_idx[0:rows, s:s + 1], axis=0),
                                        bounds_check=T - 1, oob_is_err=False).then_inc(gathered[s], 16)

            def scatter_rows(s, rows):
                pool.indirect_dma_start(y_dram, bass.IndirectOffsetOnAxis(ap=sca_idx[0:rows, s:s + 1], axis=0),
                                        ye[s][0:rows, :], None, bounds_check=2 * T - 1, oob_is_err=False
                                        ).then_inc(scattered[s], 16)

            def gather(b, n, i, s):
                size = size_class(b)
                n_1, freed = pool.to_reg(n + 1), pool.to_reg(i + 1)
                pool.wait_ge(np_ready, 1)
                pool.wait_ge(xT_done[s], freed)
                pool.tensor_copy(gat_idx[:, s:s + 1], tok_tab[:, bass.ds(b, 1)] if not isinstance(b, int)
                                 else tok_tab[:, b:b + 1]).then_inc(gidx_copied, 1)
                pool.wait_ge(h2_stored, 16 * NT)
                pool.wait_ge(gidx_copied, n_1)
                by_size(size, gather_rows, s)

            def scatter(b, n, i, s):
                size = size_class(b)
                n_1, n_2 = pool.to_reg(n + 1), pool.to_reg(n + 2)
                pool.tensor_copy(sca_idx[:, s:s + 1], id_tab[:, bass.ds(b, 1)] if not isinstance(b, int)
                                 else id_tab[:, b:b + 1]).then_inc(sidx_copied, 1)
                pool.wait_ge(np_ready, 1)
                pool.wait_ge(sidx_copied, n_1)
                for h in range(2):
                    pool.wait_ge(ye_ready[h], n_2)
                by_size(size, scatter_rows, s)

            def free_rows(i, s):
                landed = pool.to_reg(16 * i + 16)
                pool.wait_ge(np_ready, 1)
                pool.wait_ge(scattered[s], landed)
                pool.sem_inc(ye_free[s], 1)

            n_pass = passes(pool)
            with pool.Fori(0, n_pass) as p:
                n0, i0 = NE * p, (NE // 2) * p
                tables, flags = pool.to_reg(2 * p + 2), pool.to_reg(4 * p + 5)
                pool.wait_ge(np_ready, 1)
                pool.wait_ge(tab_ready, tables)
                pool.wait_ge(totals, flags)
                for k in range(5):
                    gather(k, n0 + k, i0 + k // 2, k % 2)
                scatter(0, n0, i0, 0)
                with pool.Fori(0, NE // 2 - 3) as i:
                    gather(2 * i + 5, n0 + 2 * i + 5, i0 + i + 2, 1)
                    scatter(2 * i + 1, n0 + 2 * i + 1, i0 + i, 1)
                    free_rows(i0 + i, 0)
                    gather(2 * i + 6, n0 + 2 * i + 6, i0 + i + 3, 0)
                    scatter(2 * i + 2, n0 + 2 * i + 2, i0 + i + 1, 0)
                    free_rows(i0 + i, 1)
                gather(NE - 1, n0 + NE - 1, i0 + NE // 2 - 1, 1)
                for k in range(NE - 5, NE):
                    scatter(k, n0 + k, i0 + k // 2, k % 2)
                    free_rows(i0 + (k - 1) // 2, (k - 1) % 2)
                free_rows(i0 + NE // 2 - 1, 1)
                pool.sem_inc(pass_closed, 1)
            for t in range(NT):
                pool.wait_ge(fms, t + 1)
                pool.tensor_tensor(rst[:, t:t + 1], msq[:, t:t + 1], mhalf[:, 0:1], ALU.pow).then_inc(frs, 1)

        @block.tensor
        def _(pe):
            for s_ in (vT_done, z_done, *xT_done, *unit_used, hidT_ps, *down_done):
                pe.sem_inc(s_, 1)
            pe.wait_ge(consts, 10)

            def project(j, k, first=False):
                pe.wait_ge(in_lo_done, KINDS * j + k + 1)
                for c in range(NC):
                    if first:
                        pe.wait_ge(h_lo_done, c + 1)
                    for w, h in ((in_hi, h_hi), (in_hi, h_lo), (in_lo, h_hi)):
                        last = pe.matmul(bank[k], w[k][:, c * P:(c + 1) * P], h[:, c, :],
                                         start=(c == 0 and w is in_hi and h is h_hi),
                                         stop=(c == NC - 1 and w is in_lo))
                last.then_inc(proj_done, 1)

            def transpose_v(j):
                pe.wait_ge(v_gelu, j + 1)
                pe.wait_ge(vhat_ready, j + 1)
                for n in range(NT):
                    last = pe.transpose(bank[7][:, n * P:(n + 1) * P], g_v[:, n * P:(n + 1) * P], ident[:])
                last.then_inc(vT_done, 1)

            def gate_z(j):
                pe.wait_ge(vhat_ready, j + 2)
                w_sp_j = (w_sp[:, j, :] if isinstance(j, int)
                          else w_sp[:, bass.ds(j, 1), :].rearrange("p o q -> p (o q)"))
                for n in range(NT):
                    last = pe.matmul(bank[0][:, n * P:(n + 1) * P], vhat[:, n * P:(n + 1) * P], w_sp_j,
                                     start=True, stop=True)
                last.then_inc(z_done, 1)

            project(0, V_, first=True)
            project(0, U_)
            pe.wait_ge(squares_summed, NC - 1)
            for n in range(NT):
                last = pe.matmul(bank[7][:, n:n + 1], sq_sum[:, n * P:(n + 1) * P], ones[:, 0:1], start=True, stop=True)
            last.then_inc(ms_summed, 1)
            project(0, CC_)
            for n in range(NT):
                pe.wait_ge(diag_ready, n + 1)
                last = pe.matmul(bank[7][:, n * P:(n + 1) * P], ones[:], rms_diag[:, n, :], start=True, stop=True)
            last.then_inc(rms_spread, 1)
            project(0, XC_)
            transpose_v(0)
            project(0, CB_)
            gate_z(0)
            project(0, GB_)
            project(0, GA_)
            with pe.Fori(1, NJ) as j:
                pe.wait_ge(zb_done, j + 1)
                project(j, V_)
                pe.wait_ge(u_scaled, j + 1)
                project(j, U_)
                transpose_v(j)
                pe.wait_ge(cc_scaled, j + 1)
                project(j, CC_)
                gate_z(j)
                for k, free in ((XC_, conv_in), (CB_, yb_done), (GB_, b_scaled), (GA_, a_scaled)):
                    pe.wait_ge(free, j + 1)
                    project(j, k)

            def out_proj(t, halves=(0, 1)):
                if t >= 2 and halves[0] == 0:
                    pe.wait_ge(x2_ready, 2 * (t - 2) + 2)
                order = [k for k in range(NC) if k != GA_] + [GA_]
                if t == 0:
                    steps = [(k, h) for k in order for h in range(2)]
                else:
                    steps = [(k, h) for h in halves for k in order]
                for k, h in steps:
                    if t == 0 and h == 0:
                        pe.wait_ge(in_lo_done, KINDS * NJ + (k + 1 if k < GA_ else k if k > GA_ else NC))
                        pe.wait_ge(m_lo_done, k + 1)
                    rows = slice(t * P, (t + 1) * P)
                    cols = slice(h * HALF, (h + 1) * HALF)
                    for i, (m, w) in enumerate(((m_hi[:, k, rows], in_hi[k]), (m_hi[:, k, rows], in_lo[k]),
                                                (m_lo[k][:, rows], in_hi[k]))):
                        last = pe.matmul(bank[2 * (t % 2) + h], m, w[:, cols], start=(k == order[0] and i == 0),
                                         stop=(k == order[-1] and i == 2))
                    if k == order[-1]:
                        last.then_inc(o_done, 1)

            def h2_transposes(t):
                pe.wait_ge(h2_ready, t + 1)
                for h in range(2):
                    if t >= 1:
                        pe.wait_ge(h2T_ready, 2 * t - 1 + h)
                    for c in range(4):
                        last = pe.transpose(bank[4 + h][:, c * P:(c + 1) * P], h2p[:, t, 4 * h + c, :], ident[:])
                    last.then_inc(h2T_ps, 1)

            def router_logits(t):
                if t == 0:
                    pe.wait_ge(wr_in, 32)
                if t >= 1:
                    pe.wait_ge(logits_read, t)
                for c in range(NC):
                    if c % 4 == 0:
                        pe.wait_ge(h2T_ready, 2 * t + c // 4 + 1)
                    last = pe.matmul(bank[6][:, 0:NG + NE], h2T[:, c, :], wr[:, c, :], start=(c == 0),
                                     stop=(c == NC - 1))
                last.then_inc(logits, 1)

            def prefix(t):
                pe.wait_ge(member_ready, t + 1)
                for q in range(t + 1):
                    last = pe.matmul(bank[7][:, t * NE:(t + 1) * NE], upper[:] if q == t else ones_r[:],
                                     member[:, q, :], start=(q == 0), stop=(q == t))
                if t == NT - 1:
                    for q in range(NT):
                        last = pe.matmul(bank[7][:, NT * NE:(NT + 1) * NE], ones_r[:], member[:, q, :],
                                         start=(q == 0), stop=(q == NT - 1))
                last.then_inc(prefix_done, 1)

            pe.wait_ge(zb_done, NJ + 1)
            pe.wait_ge(u_scaled, NJ + 1)
            out_proj(0)
            out_proj(1)
            h2_transposes(0)
            out_proj(2, (0,))
            router_logits(0)
            out_proj(2, (1,))
            prefix(0)
            h2_transposes(1)
            out_proj(3, (0,))
            router_logits(1)
            h2_transposes(2)
            out_proj(3, (1,))
            prefix(1)
            router_logits(2)
            h2_transposes(3)
            router_logits(3)
            prefix(2)
            prefix(3)

            def transpose_rows(i, s):
                landed = pe.to_reg(16 * i + 16)
                pe.wait_ge(consts, 10)
                pe.wait_ge(gathered[s], landed)
                for c in range(NC):
                    last = pe.transpose(bank[6][:, c * CAP:(c + 1) * CAP], xg[s][:, c * P:(c + 1) * P],
                                        ident[0:CAP, 0:CAP])
                last.then_inc(xT_done[s], 1)

            def product(n, s, half, b):
                for u in range(UNITS):
                    k = half * UNITS + u
                    pe.wait_ge(lo_done[k], n + 1)
                    for c in range(UC):
                        for part in (w_hi, w_lo):
                            last = pe.matmul(bank[b], xs[:, s, u * UC + c, :],
                                             part[:, k % RING, c * FE:(c + 1) * FE],
                                             start=(u == 0 and c == 0 and part is w_hi),
                                             stop=(u == UNITS - 1 and c == UC - 1 and part is w_lo))
                    last.then_inc(unit_used[k], 1)

            def hid_transposes(n):
                hid_n, copied = pe.to_reg(n + 2), pe.to_reg(n + 1)
                pe.wait_ge(consts, 10)
                pe.wait_ge(hid_ready, hid_n)
                pe.wait_ge(hidT_ready, copied)
                for c in range(NF):
                    last = pe.transpose(bank[7][:, c * CAP:(c + 1) * CAP], hid[:, c * P:(c + 1) * P],
                                        ident[0:CAP, 0:CAP])
                last.then_inc(hidT_ps, 1)

            def down(n, i, s):
                pe.wait_ge(hidT_ready, n + 2)
                for h in range(2):
                    pe.wait_ge(ye_ready[h], n + 1)
                for c in range(NF):
                    if c % (NF // 2) == 0:
                        pe.wait_ge(dn_in[2 * s + c // (NF // 2)], 16 * i + 16)
                    for h in range(2):
                        last = pe.matmul(bank[4 + h][0:CAP, :], hidT[:, c, :],
                                         dn_raw[:, s, c * D + h * HALF:c * D + (h + 1) * HALF],
                                         start=(c == 0), stop=(c == NF - 1))
                        if c == NF - 1:
                            last.then_inc(down_done[h], 1)

            def pe_block(n, i, s, has_prev, has_next, i_prev, i_next):
                pe.wait_ge(xlo_done, n + 2)
                pe.wait_ge(g_summed[s], i + 1)
                product(n, s, 0, s)
                if has_next:
                    transpose_rows(i_next, 1 - s)
                if has_prev:
                    hid_transposes(n - 1)
                pe.wait_ge(u_summed[s], i + 1)
                product(n, s, 1, 2 + s)
                if has_prev:
                    down(n - 1, i_prev, 1 - s)

            n_pass = passes(pe)
            with pe.Fori(0, n_pass) as p:
                n0, i0 = NE * p, (NE // 2) * p
                pe.wait_ge(rv_ready, 2 * NT * p + 2 * NT)
                for q in range(2 * NT):
                    last = pe.matmul(bank[7][0:CAP, 0:NE], r_all[:, q, :], v_all[:, q, :], start=(q == 0),
                                     stop=(q == 2 * NT - 1))
                last.then_inc(tab_ps, 1)
                pe.wait_ge(xlo_done, n0 + 1)
                transpose_rows(i0, 0)
                pe.wait_ge(tab_ready, 2 * p + 2)
                pe_block(n0, i0, 0, False, True, None, i0)
                with pe.Fori(0, NE // 2 - 1) as i:
                    pe_block(n0 + 2 * i + 1, i0 + i, 1, True, True, i0 + i, i0 + i + 1)
                    pe_block(n0 + 2 * i + 2, i0 + i + 1, 0, True, True, i0 + i, i0 + i + 1)
                pe_block(n0 + NE - 1, i0 + NE // 2 - 1, 1, True, False, i0 + NE // 2 - 1, None)
                hid_transposes(n0 + NE - 1)
                down(n0 + NE - 1, i0 + NE // 2 - 1, 1)

        @block.scalar
        def _(act):
            for s_ in (hidT_ready, g_act_ready, ye_ready[0]):
                act.sem_inc(s_, 1)

            def in_hi_copy(j, k):
                act.wait_ge(w_in_in[k], 16 * j + 16)
                act.activation(in_hi[k], in_raw[k], ACT.Copy).then_inc(in_hi_done, 1)

            in_hi_copy(0, V_)
            act.wait_ge(gmix_in, 16)
            for c in range(NC):
                act.wait_ge(xT_in[c // 2], 16)
                act.activation(h_hi[:, c, :], h_raw[:, c, :], ACT.Copy, scale=gmix[:, c:c + 1]).then_inc(h_hi_done, 1)
            in_hi_copy(0, U_)
            for c in range(NC):
                act.activation(squares[c], h_raw[:, c, :], ACT.Square).then_inc(squared, 1)
                if c == NC // 2:
                    in_hi_copy(0, CC_)
            for k in range(XC_, GA_):
                in_hi_copy(0, k)
            act.wait_ge(rms_spread, 1)
            act.activation(rms_all, bank[7], ACT.Copy).then_inc(rms_copied, 1)

            def mix_act(j):
                in_hi_copy(j, GA_)
                act.wait_ge(v_scaled, j + 1)
                act.activation(g_v, g_v, ACT.Gelu_apprx_tanh).then_inc(v_gelu, 1)
                act.wait_ge(u_scaled, j + 2)
                act.activation(g_u, g_u, ACT.Gelu_apprx_tanh).then_inc(u_gelu, 1)
                for k in (V_, U_, CC_, XC_):
                    in_hi_copy(j + 1, k)
                act.wait_ge(b_scaled, j + 2)
                act.activation(t_b, t_b, ACT.Tanh, scale=0.5).then_inc(tanh_b, 1)
                in_hi_copy(j + 1, CB_)
                act.wait_ge(a_scaled, j + 2)
                act.activation(t_a, t_a, ACT.Tanh, scale=0.5).then_inc(tanh_a, 1)
                in_hi_copy(j + 1, GB_)
                act.wait_ge(merged_done, j + 1)
                act.activation(m_hi[:, bass.ds(j, 1), :].rearrange("p o t -> p (o t)"), cnv, ACT.Copy
                               ).then_inc(m_hi_done, 1)

            with act.Fori(0, NJ) as j:
                mix_act(j)
            act.wait_ge(w_in_in[KINDS], 16)
            act.activation(in_hi[KINDS], in_raw[KINDS], ACT.Copy).then_inc(in_hi_done, 1)
            in_hi_copy(NJ, GA_)

            def act_square(t):
                act.wait_ge(x2_ready, 2 * t + 2)
                if t >= 1:
                    act.wait_ge(ssq_ready, t)
                act.activation(sq_dump, resid[:, t, :], ACT.Square, accum_out=ssq[:, t:t + 1]
                               ).then_inc(ssq_ready, 1)

            def act_h2T(t):
                for h in range(2):
                    act.wait_ge(h2T_ps, 2 * t + h + 1)
                    if t >= 1 and h == 0:
                        act.wait_ge(logits, t)
                    act.activation(h2T[:, 4 * h:4 * h + 4, :].rearrange("p c q -> p (c q)"),
                                   bank[4 + h], ACT.Copy).then_inc(h2T_ready, 1)

            def act_exps(t):
                act.wait_ge(ngm_ready, t + 1)
                act.activation(gexp[:], lg[:, 0:NG], ACT.Exp, bias=ngm[:], accum_out=gsum_e[:]).then_inc(gexp_done, 1)
                act.wait_ge(e2_ready, t + 1)
                act.activation(e2[:], eif[:, 0:1], ACT.Exp).then_inc(e2_done, 1)

            act_square(0)
            act_square(1)
            act_h2T(0)
            act_exps(0)
            act_h2T(1)
            act_square(2)
            act_exps(1)
            act_h2T(2)
            act_square(3)
            act_h2T(3)
            act_exps(2)
            act_exps(3)

            def hi_unit(n, i, s, half, u):
                k = half * UNITS + u
                if u == 0:
                    act.wait_ge(gu_in[2 * s + half], 16 * i + 16)
                if k >= RING:
                    act.wait_ge(unit_used[k - RING], n + 2)
                else:
                    act.wait_ge(unit_used[k + RING], n + 1)
                act.activation(w_hi[:, k % RING, :], gu_raw[:, 2 * s + half, u * UC * FE:(u + 1) * UC * FE],
                               ACT.Copy).then_inc(hi_done, 1)

            def x_hi(n, i, s):
                act.wait_ge(xT_done[s], i + 2)
                act.activation(xs[:, s, :, 0:CAP], bank[6].rearrange("p (c r) -> p c r", c=NC), ACT.Copy
                               ).then_inc(xhi_done, 1)

            def hid_copy(n):
                act.wait_ge(hidT_ps, n + 2)
                act.wait_ge(down_done[1], n + 1)
                act.activation(hidT[:, :, :].rearrange("p c r -> p (c r)"), bank[7][:, 0:NF * CAP], ACT.Copy
                               ).then_inc(hidT_ready, 1)

            def y_half(n, i, s):
                act.wait_ge(down_done[0], n + 2)
                act.wait_ge(ye_free[s], i + 1)
                act.activation(ye[s][:, 0:HALF], bank[4][0:CAP, :], ACT.Copy).then_inc(ye_ready[0], 1)

            def act_block(n, i, s, has_prev, has_next, i_prev, i_next):
                for u in range(UNITS):
                    hi_unit(n, i, s, 1, u)
                act.wait_ge(unit_used[UNITS - 1], n + 2)
                if has_prev:
                    act.wait_ge(g_summed[1 - s], i_prev + 2)
                act.activation(g_low, bank[s][CAP:2 * CAP, :], ACT.Copy).then_inc(g_low_ready, 1)
                if has_next:
                    x_hi(n + 1, i_next, 1 - s)
                if has_prev:
                    hid_copy(n - 1)
                if has_next:
                    hi_unit(n + 1, i_next, 1 - s, 0, 0)
                act.wait_ge(g_summed[s], i + 2)
                act.wait_ge(hid_ready, n + 1)
                act.activation(g_act, g_sum, ACT.Silu).then_inc(g_act_ready, 1)
                if has_next:
                    for u in range(1, UNITS):
                        hi_unit(n + 1, i_next, 1 - s, 0, u)
                act.wait_ge(unit_used[2 * UNITS - 1], n + 2)
                if has_prev:
                    act.wait_ge(u_summed[1 - s], i_prev + 2)
                act.activation(u_low, bank[2 + s][CAP:2 * CAP, :], ACT.Copy).then_inc(u_low_ready, 1)
                if has_prev:
                    y_half(n - 1, i_prev, 1 - s)

            n_pass = passes(act)
            with act.Fori(0, n_pass) as p:
                n0, i0 = NE * p, (NE // 2) * p
                for u in range(UNITS):
                    hi_unit(n0, i0, 0, 0, u)
                x_hi(n0, i0, 0)
                act_block(n0, i0, 0, False, True, None, i0)
                with act.Fori(0, NE // 2 - 1) as i:
                    act_block(n0 + 2 * i + 1, i0 + i, 1, True, True, i0 + i, i0 + i + 1)
                    act_block(n0 + 2 * i + 2, i0 + i + 1, 0, True, True, i0 + i, i0 + i + 1)
                act_block(n0 + NE - 1, i0 + NE // 2 - 1, 1, True, False, i0 + NE // 2 - 1, None)
                hid_copy(n0 + NE - 1)
                y_half(n0 + NE - 1, i0 + NE // 2 - 1, 1)

            for t in range(NT):
                act.wait_ge(comb1, t + 1)
                if t >= 1:
                    act.wait_ge(fsq, t)
                act.activation(sq_dump, resid[:, t, :], ACT.Square, accum_out=ssq[:, t:t + 1]).then_inc(fsq, 1)

        @block.vector
        def _(dve):
            for s_ in (zb_done, vhat_ready, conv_in, yb_done, u_scaled, cc_scaled, b_scaled, a_scaled, xlo_done,
                       *g_summed, *u_summed, hid_ready, ye_ready[1]):
                dve.sem_inc(s_, 1)

            def in_lo_sub(j, k):
                dve.wait_ge(in_hi_done, KINDS * j + k + 1)
                dve.tensor_tensor(in_lo[k], in_raw[k], in_hi[k].bitcast(F32), ALU.subtract
                                  ).then_inc(in_lo_done, 1)

            in_lo_sub(0, V_)
            dve.wait_ge(gmix_in, 16)
            for c in range(NC):
                dve.wait_ge(h_hi_done, c + 1)
                dve.scalar_tensor_tensor(h_lo[:, c, :], h_raw[:, c, :], gmix[:, c:c + 1], h_hi[:, c, :].bitcast(F32),
                                         ALU.mult, ALU.subtract).then_inc(h_lo_done, 1)
            in_lo_sub(0, U_)
            for c in range(1, NC):
                dve.wait_ge(squared, c + 1)
                if c >= 2:
                    dve.wait_ge(squares_summed, c - 1)
                dve.tensor_tensor(sq_sum, sq_sum, squares[c], ALU.add).then_inc(squares_summed, 1)
                if c == NC // 2:
                    in_lo_sub(0, CC_)
            dve.wait_ge(ms_summed, 1)
            dve.tensor_scalar(msq[:], bank[7][:, 0:NT], 1.0 / D, EPS, ALU.mult, ALU.add).then_inc(ms_ready, 1)
            dve.wait_ge(rms_ready, 1)
            for n in range(NT):
                dve.tensor_scalar(rms_diag[:, n, :], ident[:], rst[:, n:n + 1], None, ALU.mult
                                  ).then_inc(diag_ready, 1)
            for k in range(XC_, GA_):
                in_lo_sub(0, k)
            dve.wait_ge(rms_copied, 1)
            dve.tensor_tensor(rms_sq, rms_all, rms_all, ALU.mult).then_inc(rms_squared, 1)
            dve.wait_ge(rms_squared, 1)
            dve.wait_ge(small_in, 64)

            def scaled(j, k, tile, done):
                dve.wait_ge(proj_done, KINDS * j + k + 1)
                dve.tensor_tensor(tile, bank[k], rms_sq if k == CC_ else rms_all, ALU.mult).then_inc(done, 1)

            def mix_dve(j, j0, m_lo_half):
                dve.tensor_copy(par[:, 0:3], wconv[:, bass.ds(j, 1), :].rearrange("p o k -> p (o k)")
                                ).then_inc(par_ready, 1)
                dve.tensor_copy(par[:, 3:4], gsgu[:, bass.ds(j, 1)]).then_inc(par_ready, 1)
                in_lo_sub(j, GA_)
                scaled(j, V_, g_v, v_scaled)
                scaled(j, U_, g_u, u_scaled)
                dve.wait_ge(vT_done, j + 2)
                for n in range(NT):
                    last = dve.bn_stats(bnst[:, n, :], bank[7][:, n * P:(n + 1) * P])
                last.then_inc(stats, 1)
                stats_j = dve.to_reg(j + 1)
                dve.wait_ge(consts, 10)
                dve.wait_ge(stats, stats_j)
                for n in range(NT):
                    last = dve.bn_aggr(bnmv[:, n, :], bnst[:, n, :])
                last.then_inc(aggr, 1)
                dve.wait_ge(aggr, j + 1)
                dve.tensor_scalar(lnv[:], bnmv[:, :, 1], EPS, None, ALU.add).then_inc(var_eps, 1)
                dve.wait_ge(ln_rstd, j + 1)
                dve.wait_ge(z_done, j + 1)
                for n in range(NT):
                    last = dve.tensor_scalar(vhat[:, n * P:(n + 1) * P], bank[7][:, n * P:(n + 1) * P],
                                             bnmv[:, n, 0:1], lnr[:, n:n + 1], ALU.subtract, ALU.mult)
                last.then_inc(vhat_ready, 1)
                in_lo_sub(j + 1, V_)
                scaled(j, CC_, c_c, cc_scaled)
                dve.wait_ge(z_done, j + 2)
                dve.wait_ge(par_ready, 2 * j + 2)
                for n in range(NT):
                    last = dve.scalar_tensor_tensor(a_z[:, n * P:(n + 1) * P], bank[0][:, n * P:(n + 1) * P],
                                                    par[:, 3:4],
                                                    b_sp[:, bass.ds(j, 1), :].rearrange("p o q -> p (o q)"),
                                                    ALU.mult, ALU.add)
                last.then_inc(zb_done, 1)
                dve.wait_ge(zb_done, j + 2)
                dve.wait_ge(u_gelu, j + 1)
                dve.tensor_tensor(a_z, a_z, g_u, ALU.mult).then_inc(az_done, 1)
                in_lo_sub(j + 1, U_)
                dve.wait_ge(cc_scaled, j + 2)
                dve.wait_ge(proj_done, KINDS * j + XC_ + 1)
                dve.tensor_tensor(zc[:, 1:T + 1], bank[3], c_c, ALU.mult).then_inc(conv_in, 1)
                dve.wait_ge(conv_in, j + 2)
                dve.tensor_scalar(cnv, zc[:, 0:T], par[:, 0:1], None, ALU.mult).then_inc(conv0, 1)
                dve.wait_ge(conv0, j + 1)
                dve.scalar_tensor_tensor(cnv, zc[:, 1:T + 1], par[:, 1:2], cnv, ALU.mult, ALU.add).then_inc(conv1, 1)
                dve.wait_ge(conv1, j + 1)
                dve.scalar_tensor_tensor(cnv, zc[:, 2:T + 2], par[:, 2:3], cnv, ALU.mult, ALU.add).then_inc(conv2, 1)
                dve.wait_ge(conv2, j + 1)
                dve.tensor_tensor(cnv, cnv, rms_all, ALU.mult).then_inc(cb_scaled, 1)
                in_lo_sub(j + 1, CC_)
                dve.wait_ge(cb_scaled, j + 1)
                dve.wait_ge(proj_done, KINDS * j + CB_ + 1)
                dve.tensor_tensor(cnv, bank[4], cnv, ALU.mult).then_inc(yb_done, 1)
                in_lo_sub(j + 1, XC_)
                scaled(j, GB_, t_b, b_scaled)
                in_lo_sub(j + 1, CB_)
                dve.wait_ge(yb_done, j + 2)
                dve.wait_ge(tanh_b, j + 1)
                dve.scalar_tensor_tensor(cnv, t_b, 1.0, cnv, ALU.add, ALU.mult).then_inc(b_gated, 1)
                scaled(j, GA_, t_a, a_scaled)
                dve.wait_ge(az_done, j + 1)
                dve.wait_ge(tanh_a, j + 1)
                dve.scalar_tensor_tensor(a_z, t_a, 1.0, a_z, ALU.add, ALU.mult).then_inc(a_gated, 1)
                dve.wait_ge(b_gated, j + 1)
                dve.wait_ge(a_gated, j + 1)
                dve.tensor_tensor(cnv, a_z, cnv, ALU.add).then_inc(merged_done, 1)
                in_lo_sub(j + 1, GB_)
                dve.wait_ge(m_hi_done, j + 1)
                dve.tensor_tensor(m_lo_half[:, bass.ds(j - j0, 1), :].rearrange("p o t -> p (o t)"), cnv,
                                  m_hi[:, bass.ds(j, 1), :].bitcast(F32).rearrange("p o t -> p (o t)"), ALU.subtract
                                  ).then_inc(m_lo_done, 1)

            with dve.Fori(0, NJ // 2) as j:
                mix_dve(j, 0, m_lo_a)
            with dve.Fori(NJ // 2, NJ) as j:
                mix_dve(j, NJ // 2, m_lo_b)
            dve.wait_ge(in_hi_done, KINDS * NJ + KINDS)
            dve.tensor_tensor(in_lo[KINDS], in_raw[KINDS], in_hi[KINDS].bitcast(F32), ALU.subtract
                              ).then_inc(in_lo_done, 1)
            dve.wait_ge(in_hi_done, KINDS * NJ + NC)
            dve.tensor_tensor(in_lo[GA_], in_raw[GA_], in_hi[GA_].bitcast(F32), ALU.subtract).then_inc(in_lo_done, 1)

            step = [0]

            def link(ins):
                step[0] += 1
                ins.then_inc(rstep, 1)
                dve.wait_ge(rstep, step[0])

            def residual(t, ranks_of=None):
                if t == 0:
                    dve.wait_ge(x_in, 16)
                for h in range(2):
                    dve.wait_ge(o_done, 2 * t + h + 1)
                    dve.scalar_tensor_tensor(resid[:, t, h * HALF:(h + 1) * HALF], bank[2 * (t % 2) + h], 0.5,
                                             resid[:, t, h * HALF:(h + 1) * HALF], ALU.mult, ALU.add
                                             ).then_inc(x2_ready, 1)
                if ranks_of is not None:
                    rank_of(ranks_of)
                dve.wait_ge(ssq_ready, t + 1)
                dve.tensor_scalar(msq[:, t:t + 1], ssq[:, t:t + 1], 1.0 / D, EPS, ALU.mult, ALU.add
                                  ).then_inc(msq_ready, 1)
                dve.wait_ge(gffn_in, 16)
                dve.wait_ge(rst_ready, t + 1)
                dve.scalar_tensor_tensor(h2p[:, t, :, :].rearrange("p c q -> p q c"),
                                         resid[:, t, :].rearrange("p (q c) -> p q c", c=NC), rst[:, t:t + 1],
                                         gffn.rearrange("p (q c) -> p q c", c=NC), ALU.mult, ALU.mult
                                         ).then_inc(h2_ready, 1)

            def rank_onehot(t):
                for k in range(2):
                    dve.tensor_scalar(r_all[:, 2 * t + k, :], iota_r[:], rank[:, t, k:k + 1], None, ALU.is_equal
                                      ).then_inc(rv_ready, 1)

            def route(t, ranks_of=None):
                dve.wait_ge(logits, t + 1)
                if t >= 1:
                    dve.wait_ge(e2_done, t)
                dve.tensor_copy(lg[:], bank[6][:, 0:NG + NE]).then_inc(logits_read, 1)
                dve.wait_ge(logits_read, t + 1)
                link(dve.max(gmax[:], lg[:, 0:NG]))
                dve.tensor_scalar(ngm[:], gmax[:, 0:1], -1.0, None, ALU.mult).then_inc(ngm_ready, 1)
                link(dve.max_index(gidx[:], gmax[:], lg[:, 0:NG]))
                link(dve.tensor_copy(gidf[:], gidx[:, 0:1]))
                link(dve.tensor_scalar(gmask[:], iota_e[:, 0:NG], gidf[:], None, ALU.is_equal))
                link(dve.tensor_tensor(elm[:].rearrange("p (g e) -> p g e", g=NG),
                                       lg[:, NG:NG + NE].rearrange("p (g e) -> p g e", g=NG),
                                       gmask[:].unsqueeze(2).to_broadcast([P, NG, NE // NG]), ALU.mult))
                link(dve.tensor_reduce(el8[:], elm[:].rearrange("p (g e) -> p e g", g=NG), AX.X, ALU.add))
                link(dve.max(em8[:], el8[:]))
                link(dve.max_index(ei8[:], em8[:], el8[:]))
                link(dve.tensor_copy(eif[:], ei8[:, 0:2]))
                link(dve.scalar_tensor_tensor(eid[:, t, :], gidf[:].to_broadcast([P, 2]), float(NE // NG), eif[:],
                                              ALU.mult, ALU.add))
                if ranks_of is not None:
                    rank_of(ranks_of)
                for k in range(2):
                    link(dve.tensor_scalar(onehot[:, k, :], iota_e[:], eid[:, t, k:k + 1], None, ALU.is_equal))
                dve.tensor_tensor(member[:, t, :], onehot[:, 0, :], onehot[:, 1, :], ALU.add
                                  ).then_inc(member_ready, 1)
                dve.tensor_tensor(eif[:, 0:1], em8[:, 1:2], em8[:, 0:1], ALU.subtract).then_inc(e2_ready, 1)
                for k in range(2):
                    link(dve.tensor_scalar(v_all[:, 2 * t + k, :], iota_e[:], eid[:, t, k:k + 1], idv[:, t, k:k + 1],
                                           ALU.is_equal, ALU.mult))
                dve.wait_ge(gexp_done, t + 1)
                dve.wait_ge(e2_done, t + 1)
                link(dve.tensor_scalar(den[:], e2[:], 1.0, gsum_e[:], ALU.add, ALU.mult))
                link(dve.reciprocal(gate_w[:, t, 0:1], den[:]))
                dve.tensor_tensor(gate_w[:, t, 1:2], gate_w[:, t, 0:1], e2[:], ALU.mult).then_inc(weights_ready, 1)

            def rank_of(t):
                dve.wait_ge(prefix_done, t + 1)
                if t == NT - 1:
                    link(dve.tensor_reduce(cmax[:], bank[7][:, NT * NE:(NT + 1) * NE], AX.X, ALU.max))
                    link(dve.tensor_scalar(thrm[:], thr[:], cmax[:], None, ALU.is_lt))
                    link(dve.tensor_reduce(npf[:], thrm[:], AX.X, ALU.add))
                    dve.tensor_copy(npi[:], npf[:]).then_inc(np_ready, 1)
                    dve.tensor_copy(total[:], bank[7][0:1, NT * NE:(NT + 1) * NE]).then_inc(totals, 1)
                for k in range(2):
                    link(dve.tensor_tensor_reduce(elm[:], bank[7][:, t * NE:(t + 1) * NE], onehot[:, k, :],
                                                  1.0, 0.0, ALU.mult, ALU.add, rank[:, t, k:k + 1]))
                rank_onehot(t)

            residual(0)
            residual(1)
            route(0)
            residual(2, 0)
            route(1)
            residual(3, 1)
            route(2)
            route(3, 2)
            rank_of(3)

            def lo_unit(n, i, s, half, u):
                k = half * UNITS + u
                dve.wait_ge(hi_done, 2 * UNITS * n + k + 1)
                dve.tensor_tensor(w_lo[:, k % RING, :], gu_raw[:, 2 * s + half, u * UC * FE:(u + 1) * UC * FE],
                                  w_hi[:, k % RING, :].bitcast(F32), ALU.subtract).then_inc(lo_done[k], 1)

            def x_lo(n, s):
                dve.wait_ge(xhi_done, n + 1)
                dve.tensor_tensor(xs[:, s, :, CAP:2 * CAP], bank[6].rearrange("p (c r) -> p c r", c=NC),
                                  xs[:, s, :, 0:CAP].bitcast(F32), ALU.subtract).then_inc(xlo_done, 1)

            def y_half(n, i, s):
                dve.wait_ge(down_done[1], n + 2)
                dve.wait_ge(ye_free[s], i + 1)
                dve.tensor_copy(ye[s][:, HALF:D], bank[5][0:CAP, :]).then_inc(ye_ready[1], 1)

            def dve_block(n, i, s, has_prev, has_next, i_prev, i_next):
                for u in range(UNITS):
                    lo_unit(n, i, s, 1, u)
                dve.wait_ge(g_low_ready, n + 1)
                dve.wait_ge(g_act_ready, n + 1)
                dve.tensor_tensor(g_sum, bank[s][0:CAP, :], g_low, ALU.add).then_inc(g_summed[s], 1)
                if has_next:
                    x_lo(n + 1, 1 - s)
                    for u in range(UNITS):
                        lo_unit(n + 1, i_next, 1 - s, 0, u)
                dve.wait_ge(u_low_ready, n + 1)
                dve.tensor_tensor(u_sum, bank[2 + s][0:CAP, :], u_low, ALU.add).then_inc(u_summed[s], 1)
                dve.wait_ge(u_summed[s], i + 2)
                dve.wait_ge(g_act_ready, n + 2)
                dve.wait_ge(hidT_ps, n + 1)
                dve.tensor_tensor(hid, u_sum, g_act, ALU.mult).then_inc(hid_ready, 1)
                if has_prev:
                    y_half(n - 1, i_prev, 1 - s)

            n_pass = passes(dve)
            with dve.Fori(0, n_pass) as p:
                n0, i0 = NE * p, (NE // 2) * p
                dve.wait_ge(rv_ready, 2 * NT * p + 2 * NT)
                dve.tensor_scalar(iota_r[:], iota_r[:], float(CAP), None, ALU.add).then_inc(tab_step, 1)
                dve.wait_ge(tab_ps, p + 1)
                dve.tensor_copy(tb_v[:], bank[7][0:CAP, 0:NE]).then_inc(tab_step, 1)
                dve.wait_ge(totals, 4 * p + 1)
                dve.tensor_scalar(over_1, total[:], float(SIZES[1]), None, ALU.is_gt).then_inc(totals, 1)
                dve.wait_ge(totals, 4 * p + 2)
                dve.scalar_tensor_tensor(size_f, total[:], float(SIZES[0]), over_1, ALU.is_gt, ALU.add
                                         ).then_inc(totals, 1)
                dve.wait_ge(totals, 4 * p + 3)
                dve.tensor_scalar(total[:], total[:], float(-CAP), None, ALU.add).then_inc(totals, 1)
                dve.wait_ge(tab_step, 5 * p + 2)
                dve.tensor_scalar(tb_e[:], tb_v[:], 0.5, float(OUT_OF_RANGE), ALU.is_lt, ALU.mult).then_inc(tab_step, 1)
                dve.wait_ge(tab_step, 5 * p + 3)
                dve.scalar_tensor_tensor(tb_v[:], tb_v[:], -1.0, tb_e[:], ALU.add, ALU.add).then_inc(tab_step, 1)
                dve.wait_ge(tab_step, 5 * p + 4)
                dve.wait_ge(pass_closed, p + 1)
                dve.tensor_scalar(tb_e[:], tb_v[:], float(T) - 0.5, -float(T), ALU.is_gt, ALU.mult
                                  ).then_inc(tab_step, 1)
                dve.tensor_copy(id_tab[:], tb_v[:]).then_inc(tab_ready, 1)
                dve.tensor_copy(size_i, size_f).then_inc(totals, 1)
                dve.wait_ge(tab_step, 5 * p + 5)
                dve.tensor_tensor(tok_tab[:], tb_v[:], tb_e[:], ALU.add).then_inc(tab_ready, 1)
                for u in range(UNITS):
                    lo_unit(n0, i0, 0, 0, u)
                x_lo(n0, 0)
                dve_block(n0, i0, 0, False, True, None, i0)
                with dve.Fori(0, NE // 2 - 1) as i:
                    dve_block(n0 + 2 * i + 1, i0 + i, 1, True, True, i0 + i, i0 + i + 1)
                    dve_block(n0 + 2 * i + 2, i0 + i + 1, 0, True, True, i0 + i, i0 + i + 1)
                dve_block(n0 + NE - 1, i0 + NE // 2 - 1, 1, True, False, i0 + NE // 2 - 1, None)
                y_half(n0 + NE - 1, i0 + NE // 2 - 1, 1)
                for t in range(NT):
                    rank_onehot(t)

            dve.wait_ge(gf_in, 16)

            def combine(t):
                dve.wait_ge(weights_ready, t + 1)
                dve.wait_ge(y_in[t], 16)
                dve.scalar_tensor_tensor(resid[:, t, :], gu_raw[:, t, 0:D], gate_w[:, t, 0:1], resid[:, t, :],
                                         ALU.mult, ALU.add).then_inc(comb0, 1)
                if t >= 1:
                    mean_square(t - 1)
                dve.wait_ge(comb0, t + 1)
                dve.scalar_tensor_tensor(resid[:, t, :], gu_raw[:, t, D:2 * D], gate_w[:, t, 1:2], resid[:, t, :],
                                         ALU.mult, ALU.add).then_inc(comb1, 1)

            def mean_square(t):
                dve.wait_ge(fsq, t + 1)
                dve.tensor_scalar(msq[:, t:t + 1], ssq[:, t:t + 1], 1.0 / D, EPS, ALU.mult, ALU.add).then_inc(fms, 1)

            def finish(t):
                dve.wait_ge(frs, t + 1)
                dve.scalar_tensor_tensor(dn_raw[:, 1, t * D:(t + 1) * D], resid[:, t, :], rst[:, t:t + 1], g_fin,
                                         ALU.mult, ALU.mult).then_inc(out_ready, 1)

            combine(0)
            for t in range(1, NT):
                combine(t)
                finish(t - 1)
            mean_square(NT - 1)
            finish(NT - 1)


_ORDER = (1, 0, 3, 4, 2, 6, 5)


def kernel(x, g_mix, w_in, w_s, b_s, g_sgu, w_conv, w_out, g_ffn, w_router_group, w_router_expert, w_gate, w_up,
           w_down, g_final):
    import numpy as np
    import concourse.bacc as bacc
    from concourse.bass_utils import run_bass_kernel_spmd

    x = np.asarray(x)
    arrays = {
        "xT": np.asarray(x)[0].T.reshape(P, NC, T),
        "x": x[0].reshape(NT, P, D).transpose(1, 0, 2),
        "g_mix": np.asarray(g_mix).reshape(P, NC),
        "w_in": np.asarray(w_in)[0].reshape(P, NC, KINDS, NJ, P)[:, :, list(_ORDER)].transpose(3, 0, 2, 1, 4)
                .reshape(NJ, P, KINDS, NC * P),
        "w_sT": np.asarray(w_s)[0].transpose(2, 0, 1),
        "b_s": np.asarray(b_s).reshape(NJ * P),
        "g_sgu": np.asarray(g_sgu).reshape(NJ, P).T,
        "w_conv": np.asarray(w_conv)[0].reshape(3, NJ, P).transpose(2, 1, 0),
        "w_out": np.asarray(w_out)[0].reshape(NC, P, D),
        "g_ffn": np.asarray(g_ffn).reshape(D),
        "w_rg": np.asarray(w_router_group)[0],
        "w_re": np.asarray(w_router_expert)[0],
        "w_gate": np.asarray(w_gate)[0],
        "w_up": np.asarray(w_up)[0],
        "w_down": np.asarray(w_down)[0],
        "g_final": np.asarray(g_final).reshape(D),
    }
    nc = bacc.Bacc("TRN2", target_bir_lowering=False, num_devices=1)
    feed, aps = {}, {}
    for name, a in arrays.items():
        feed["in_" + name] = np.ascontiguousarray(a)
        aps[name] = nc.dram_tensor("in_" + name, a.shape, F32, kind="ExternalInput").ap()
    h2_dram = nc.dram_tensor("h2_rows", (T, D), F32, kind="Internal").ap()
    y_dram = nc.dram_tensor("y_rows", (2 * T, D), F32, kind="Internal").ap()
    out = nc.dram_tensor("out_0", (T, D), F32, kind="ExternalOutput").ap()
    build(nc, **aps, h2_dram=h2_dram, y_dram=y_dram, out=out)
    r = run_bass_kernel_spmd(nc, [feed], core_ids=[0])
    return r.results[0]["out_0"].reshape(1, T, D)
```
